# Optimizing a Trainium2 kernel written in Bass

```python
import jax, jax.numpy as jnp
from jax import lax
import numpy as np
import math

D_MODEL = 1024
BATCH = 1
SEQ = 256
DEPTH = 2

GRID_W = 64
CTX_LEN = 256
CONV_W = 512
CONV_K = 31
CONV_GROUPS = 8
RWKV_W = D_MODEL - CONV_W
HEAD = 64
N_HEADS = RWKV_W // HEAD
DECAY_RANK = 64
ICLR_RANK = 64
GATE_RANK = 160
SHIFT_K = 3
CONV_IN = 2 * CONV_W
RWKV_IN = 3 * RWKV_W + DECAY_RANK + ICLR_RANK + GATE_RANK
IN_COLS = CONV_IN + RWKV_IN
D_FF = -(-8 * D_MODEL // (3 * 256)) * 256
RMS_EPS = 1e-6
LN_EPS = 1e-5
GN_EPS = 64e-5
DECAY_SCALE = 0.606531


def rmsnorm(x, g):
    xf = x.astype(jnp.float32)
    y = xf * lax.rsqrt(jnp.mean(xf * xf, axis=-1, keepdims=True) + RMS_EPS)
    return (y * g).astype(x.dtype)

def modulate(h, shift, scale):
    return h * (1.0 + scale) + shift

def group_norm(x, n_groups, g, b, eps):
    shp = x.shape
    xg = x.astype(jnp.float32).reshape(shp[:-1] + (n_groups, shp[-1] // n_groups))
    mu = jnp.mean(xg, axis=-1, keepdims=True)
    var = jnp.mean(jnp.square(xg - mu), axis=-1, keepdims=True)
    xg = (xg - mu) * lax.rsqrt(var + eps)
    return xg.reshape(shp) * g + b

def dwconv(x, w):
    ch = x.shape[-1]
    return lax.conv_general_dilated(
        x, w[:, None, :].astype(x.dtype), window_strides=(1,), padding="SAME",
        dimension_numbers=("NWC", "WIO", "NWC"), feature_group_count=ch)

def grid_transpose(t, rows, cols):
    b, _, ch = t.shape
    return t.reshape(b, rows, cols, ch).transpose(0, 2, 1, 3).reshape(b, rows * cols, ch)

def to_heads(t):
    return t.reshape(t.shape[:-1] + (N_HEADS, HEAD))

def conformer_conv(u, conv_w, conv_b, cnorm_g, cnorm_b):
    val, gate = jnp.split(u, 2, axis=-1)
    z = val * jax.nn.sigmoid(gate)
    z = dwconv(z, conv_w) + conv_b
    z = group_norm(z, CONV_GROUPS, cnorm_g, cnorm_b, LN_EPS)
    return jax.nn.silu(z)

def rwkv_prep(u, shift_w, decay_b0, decay_up, iclr_b0, iclr_up, k_k, k_a, g_up):
    u = dwconv(u, shift_w).astype(jnp.float32)
    o1 = 3 * RWKV_W
    o2 = o1 + DECAY_RANK
    o3 = o2 + ICLR_RANK
    r, k, v, w_lo, a_lo, g_lo = jnp.split(u, [RWKV_W, 2 * RWKV_W, o1, o2, o3], axis=-1)
    kk = to_heads(k * k_k)
    kk = kk / jnp.maximum(jnp.sqrt(jnp.sum(kk * kk, axis=-1, keepdims=True)), 1e-12)
    dirs = []
    for d in range(2):
        decay = jnp.exp(-DECAY_SCALE * jax.nn.sigmoid(decay_b0[d] + jnp.tanh(w_lo) @ decay_up[d]))
        a = jax.nn.sigmoid(iclr_b0[d] + a_lo @ iclr_up[d])
        k_d = k * (1.0 + (a - 1.0) * k_a)
        dirs.append((to_heads(k_d), to_heads(decay), to_heads(a)))
    g = jax.nn.sigmoid(g_lo) @ g_up
    return to_heads(r), to_heads(k), to_heads(v), kk, dirs, g

def wkv_scan(r, k, v, decay, kk, a, s0, reverse, emit):
    xs = tuple(jnp.swapaxes(t, 0, 1) for t in (r, k, v, decay, kk, kk * a))

    def step(s, inp):
        r_t, k_t, v_t, w_t, kk_t, b_t = inp
        sa = -jnp.einsum("bhvk,bhk->bhv", s, kk_t)
        s = (s * w_t[:, :, None, :] + sa[..., None] * b_t[:, :, None, :]
             + v_t[..., None] * k_t[:, :, None, :])
        y = jnp.einsum("bhvk,bhk->bhv", s, r_t) if emit else None
        return s, y

    s_fin, ys = lax.scan(step, s0, xs, reverse=reverse)
    return (jnp.swapaxes(ys, 0, 1) if emit else None), s_fin

def rwkv_scans(prep, s0_f, s0_b, emit):
    r, k, v, kk, dirs, g = prep
    (k_f, w_f, a_f), (k_b, w_b, a_b) = dirs
    y_f, s_f = wkv_scan(r, k_f, v, w_f, kk, a_f, s0_f, False, emit)
    y_b, s_b = wkv_scan(r, k_b, v, w_b, kk, a_b, s0_b, True, emit)
    y = (y_f + y_b) if emit else None
    return y, s_f, s_b

def rwkv_out(y, prep, r_k, gn_g, gn_b):
    r, k, v, kk, dirs, g = prep
    b, t = y.shape[:2]
    y = group_norm(y.reshape(b, t, RWKV_W), N_HEADS, gn_g, gn_b, GN_EPS)
    bonus = jnp.sum(r * k * to_heads(r_k), axis=-1, keepdims=True) * v
    return (y + bonus.reshape(b, t, RWKV_W)) * g

def swiglu(h, wg, wu, wd):
    return (jax.nn.silu(h @ wg) * (h @ wu)) @ wd

def first_inputs(seed: int = 0) -> dict:
    key = jax.random.key(seed)
    ks = iter(jax.random.split(key, 40))

    def nrm(shape, scale):
        return jax.random.normal(next(ks), shape, jnp.float32) * scale

    L = DEPTH
    shift_base = jnp.array([0.25, 1.0, 0.25], jnp.float32)[None, :, None]
    return {
        "x": nrm((BATCH, SEQ, D_MODEL), 1.0),
        "c": nrm((BATCH, D_MODEL), 1.0),
        "ctx": nrm((BATCH, CTX_LEN, D_MODEL), 1.0),
        "c_ctx": nrm((D_MODEL,), 1.0),
        "ada_w": nrm((L, D_MODEL, 6 * D_MODEL), 0.5 * D_MODEL ** -0.5),
        "ada_b": nrm((L, 6 * D_MODEL), 0.02),
        "norm1_g": 1.0 + nrm((L, D_MODEL), 0.02),
        "norm2_g": 1.0 + nrm((L, D_MODEL), 0.02),
        "w_in": nrm((L, D_MODEL, IN_COLS), D_MODEL ** -0.5),
        "conv_w": nrm((L, CONV_K, CONV_W), CONV_K ** -0.5),
        "conv_b": nrm((L, CONV_W), 0.02),
        "cnorm_g": 1.0 + nrm((L, CONV_W), 0.02),
        "cnorm_b": nrm((L, CONV_W), 0.02),
        "shift_w": shift_base + nrm((L, SHIFT_K, RWKV_IN), 0.1),
        "decay_b0": jax.random.uniform(next(ks), (L, 2, RWKV_W), jnp.float32, -6.0, 0.0),
        "decay_up": nrm((L, 2, DECAY_RANK, RWKV_W), 0.5 * DECAY_RANK ** -0.5),
        "iclr_b0": nrm((L, 2, RWKV_W), 0.5),
        "iclr_up": nrm((L, 2, ICLR_RANK, RWKV_W), 0.5 * ICLR_RANK ** -0.5),
        "k_k": 0.85 + nrm((L, RWKV_W), 0.05),
        "k_a": 1.0 + nrm((L, RWKV_W), 0.05),
        "g_up": nrm((L, GATE_RANK, RWKV_W), GATE_RANK ** -0.5),
        "r_k": nrm((L, RWKV_W), 0.1),
        "gn_g": 1.0 + nrm((L, RWKV_W), 0.02),
        "gn_b": nrm((L, RWKV_W), 0.02),
        "w_out": nrm((L, D_MODEL, D_MODEL), D_MODEL ** -0.5),
        "ffn_wg": nrm((L, D_MODEL, D_FF), D_MODEL ** -0.5),
        "ffn_wu": nrm((L, D_MODEL, D_FF), D_MODEL ** -0.5),
        "ffn_wd": nrm((L, D_FF, D_MODEL), D_FF ** -0.5),
        "final_g": 1.0 + nrm((D_MODEL,), 0.02),
    }

def first_block(x, c, ctx, c_ctx, ada_w, ada_b, norm1_g, norm2_g, w_in, conv_w, conv_b,
              cnorm_g, cnorm_b, shift_w, decay_b0, decay_up, iclr_b0, iclr_up, k_k, k_a,
              g_up, r_k, gn_g, gn_b, w_out, ffn_wg, ffn_wu, ffn_wd, final_g):
    rows = x.shape[1] // GRID_W
    batch = x.shape[0]
    s_zero = jnp.zeros((batch, N_HEADS, HEAD, HEAD), jnp.float32)
    silu_c = jax.nn.silu(c)
    silu_cc = jax.nn.silu(c_ctx)
    for l in range(DEPTH):
        last = l == DEPTH - 1
        col_major = l % 2 == 1
        mod_x = (silu_c @ ada_w[l] + ada_b[l])[:, None, :]
        sh1, sc1, gt1, sh2, sc2, gt2 = jnp.split(mod_x, 6, axis=-1)
        mod_c = silu_cc @ ada_w[l] + ada_b[l]
        csh1, csc1, cgt1, csh2, csc2, cgt2 = jnp.split(mod_c, 6, axis=-1)
        rw = (shift_w[l], decay_b0[l], decay_up[l], iclr_b0[l], iclr_up[l], k_k[l], k_a[l], g_up[l])
        cv = (conv_w[l], conv_b[l], cnorm_g[l], cnorm_b[l])
        post = (r_k[l], gn_g[l], gn_b[l])

        ux = modulate(rmsnorm(x, norm1_g[l]), sh1, sc1) @ w_in[l]
        uc = modulate(rmsnorm(ctx, norm1_g[l]), csh1, csc1) @ w_in[l]
        if col_major:
            ux = grid_transpose(ux, rows, GRID_W)

        prep_c = rwkv_prep(uc[..., CONV_IN:], *rw)
        yc, s_f, s_b = rwkv_scans(prep_c, s_zero, s_zero, emit=not last)
        prep_x = rwkv_prep(ux[..., CONV_IN:], *rw)
        yx, _, _ = rwkv_scans(prep_x, s_f, s_b, emit=True)

        mix_x = jnp.concatenate(
            [conformer_conv(ux[..., :CONV_IN], *cv), rwkv_out(yx, prep_x, *post)],
            axis=-1).astype(x.dtype)
        if col_major:
            mix_x = grid_transpose(mix_x, GRID_W, rows)
        x = x + gt1 * (mix_x @ w_out[l])

        x = x + gt2 * swiglu(modulate(rmsnorm(x, norm2_g[l]), sh2, sc2),
                             ffn_wg[l], ffn_wu[l], ffn_wd[l])

        if not last:
            mix_c = jnp.concatenate(
                [conformer_conv(uc[..., :CONV_IN], *cv), rwkv_out(yc, prep_c, *post)],
                axis=-1).astype(ctx.dtype)
            ctx = ctx + cgt1 * (mix_c @ w_out[l])
            ctx = ctx + cgt2 * swiglu(modulate(rmsnorm(ctx, norm2_g[l]), csh2, csc2),
                                      ffn_wg[l], ffn_wu[l], ffn_wd[l])
    return rmsnorm(x, final_g)


HG_HEADS = 4
HG_DK = 128
HG_DV = 128
HG_K = HG_HEADS * HG_DK
HG_V = HG_HEADS * HG_DV
HG_CHUNK = 64
SG_GROUPS = 4
SG_WIDTH = 512
SG_GROUP_DIM = SG_WIDTH // SG_GROUPS
SG_CHUNK = 128
D_FF_2 = 2816
ALPHA = (2 * DEPTH) ** 0.25
BETA = (8 * DEPTH) ** -0.25
D_IN = 2 * HG_K + 2 * HG_V + 2 * SG_WIDTH + 2 * D_MODEL
IN_SPLITS = (HG_K,
             2 * HG_K,
             2 * HG_K + HG_V,
             2 * HG_K + 2 * HG_V,
             2 * HG_K + 2 * HG_V + SG_WIDTH,
             2 * HG_K + 2 * HG_V + 2 * SG_WIDTH,
             2 * HG_K + 2 * HG_V + 2 * SG_WIDTH + D_MODEL)


def layer_norm(x, g, b):
    xf = x.astype(jnp.float32)
    mu = jnp.mean(xf, axis=-1, keepdims=True)
    var = jnp.mean(jnp.square(xf - mu), axis=-1, keepdims=True)
    y = (xf - mu) * lax.rsqrt(var + LN_EPS) * g.astype(jnp.float32) + b.astype(jnp.float32)
    return y.astype(x.dtype)

def swiglu_2(x, w13, w2):
    a, b = jnp.split(x @ w13, 2, axis=-1)
    return (jax.nn.silu(a) * b) @ w2

def hgrn2_chunkwise(q, k, i, log_f):
    B, T, H, _ = q.shape
    n_chunks = T // HG_CHUNK

    def to_chunks(a):
        return a.reshape(B, n_chunks, HG_CHUNK, H, a.shape[-1]).transpose(1, 0, 3, 2, 4)

    causal = jnp.tril(jnp.ones((HG_CHUNK, HG_CHUNK), dtype=bool))[:, :, None]

    def step(S, inp):
        q_c, k_c, i_c, lf_c = inp
        b = jnp.cumsum(lf_c, axis=-2)
        o_inter = jnp.einsum('bhtk,bhkv->bhtv', q_c * jnp.exp(b), S)
        diff = b[:, :, :, None, :] - b[:, :, None, :, :]
        decay = jnp.where(causal, jnp.exp(jnp.where(causal, diff, 0.0)), 0.0)
        scores = jnp.einsum('bhtk,bhtsk,bhsk->bhts', q_c, decay, k_c)
        o_intra = jnp.einsum('bhts,bhsv->bhtv', scores, i_c)
        b_last = b[:, :, -1:, :]
        S_new = jnp.exp(b_last[:, :, 0, :])[..., None] * S + jnp.einsum(
            'bhsk,bhsv->bhkv', k_c * jnp.exp(b_last - b), i_c)
        return S_new, o_inter + o_intra

    S0 = jnp.zeros((B, H, q.shape[-1], i.shape[-1]), jnp.float32)
    _, o = lax.scan(step, S0, (to_chunks(q), to_chunks(k), to_chunks(i), to_chunks(log_f)))
    return o.transpose(1, 0, 3, 2, 4).reshape(B, T, H, i.shape[-1])

def mixer(x, w_in, lb, hg_norm_g, sg_ln_g, sg_ln_b, sg_ws, sg_bs, w_branch_a, w_branch_b, w_out):
    B, T, _ = x.shape
    zq, zf, zi, zg, zu, zv, za, zb = jnp.split(x @ w_in, IN_SPLITS, axis=-1)

    f32 = jnp.float32
    lbf = lb.astype(f32)
    zff = zf.astype(f32)
    f = lbf + (1.0 - lbf) * jax.nn.sigmoid(zff)
    log_f = jnp.log(f)
    k = (1.0 - lbf) * jax.nn.sigmoid(-zff)
    hs = lambda a, d: a.reshape(B, T, HG_HEADS, d)
    o = hgrn2_chunkwise(hs(zq.astype(f32), HG_DK), hs(k, HG_DK),
                        hs(zi.astype(f32), HG_DV), hs(log_f, HG_DK))
    o = o * lax.rsqrt(jnp.mean(jnp.square(o), axis=-1, keepdims=True) + RMS_EPS)
    o = o * hg_norm_g.astype(f32).reshape(HG_HEADS, HG_DV)
    o = o.reshape(B, T, HG_V).astype(x.dtype) * jax.nn.silu(zg)
    y_a = o @ w_branch_a

    u = jax.nn.gelu(zu)
    v = layer_norm(jax.nn.gelu(zv), sg_ln_g, sg_ln_b)
    n_chunks = T // SG_CHUNK
    v = v.reshape(B, n_chunks, SG_CHUNK, SG_GROUPS, SG_GROUP_DIM)
    ws = sg_ws * jnp.tril(jnp.ones((SG_CHUNK, SG_CHUNK), sg_ws.dtype))
    mixed = jnp.einsum('gts,bnsgc->bntgc', ws, v) + sg_bs.T[None, None, :, :, None]
    y_b = (u * mixed.reshape(B, T, SG_WIDTH)) @ w_branch_b

    y = jax.nn.sigmoid(za) * y_a + jax.nn.sigmoid(zb) * y_b
    return y @ w_out

def second_inputs(seed: int = 0) -> dict:
    key = jax.random.key(seed)
    ks = jax.random.split(key, 20)
    n = jax.random.normal
    f32 = jnp.float32
    return {
        "x": n(ks[0], (BATCH, SEQ, D_MODEL), f32),
        "ffn1_w13": n(ks[1], (DEPTH, D_MODEL, 2 * D_FF_2), f32) * D_MODEL ** -0.5,
        "ffn1_w2": n(ks[2], (DEPTH, D_FF_2, D_MODEL), f32) * (D_FF_2 ** -0.5 * BETA),
        "ffn2_w13": n(ks[3], (DEPTH, D_MODEL, 2 * D_FF_2), f32) * D_MODEL ** -0.5,
        "ffn2_w2": n(ks[4], (DEPTH, D_FF_2, D_MODEL), f32) * (D_FF_2 ** -0.5 * BETA),
        "ln_g": 1.0 + 0.02 * n(ks[5], (DEPTH, 3, D_MODEL), f32),
        "ln_b": 0.02 * n(ks[6], (DEPTH, 3, D_MODEL), f32),
        "w_in": n(ks[7], (DEPTH, D_MODEL, D_IN), f32) * D_MODEL ** -0.5,
        "hg_lb": 0.5 * n(ks[8], (DEPTH, HG_K), f32),
        "hg_norm_g": 1.0 + 0.02 * n(ks[9], (DEPTH, HG_V), f32),
        "sg_ln_g": 1.0 + 0.02 * n(ks[10], (DEPTH, SG_WIDTH), f32),
        "sg_ln_b": 0.02 * n(ks[11], (DEPTH, SG_WIDTH), f32),
        "sg_ws": n(ks[12], (DEPTH, SG_GROUPS, SG_CHUNK, SG_CHUNK), f32) * SG_CHUNK ** -0.5,
        "sg_bs": 1.0 + 0.1 * n(ks[13], (DEPTH, SG_GROUPS, SG_CHUNK), f32),
        "w_branch_a": n(ks[14], (DEPTH, HG_V, D_MODEL), f32) * (HG_V ** -0.5 * BETA),
        "w_branch_b": n(ks[15], (DEPTH, SG_WIDTH, D_MODEL), f32) * (SG_WIDTH ** -0.5 * BETA),
        "w_out": n(ks[16], (DEPTH, D_MODEL, D_MODEL), f32) * (D_MODEL ** -0.5 * BETA),
    }

def second_block(x, ffn1_w13, ffn1_w2, ffn2_w13, ffn2_w2, ln_g, ln_b, w_in, hg_lb, hg_norm_g,
              sg_ln_g, sg_ln_b, sg_ws, sg_bs, w_branch_a, w_branch_b, w_out):
    lb_soft = jax.nn.softmax(hg_lb.astype(jnp.float32), axis=0)
    lower_bounds = jnp.cumsum(lb_soft, axis=0) - lb_soft[0]
    for l in range(DEPTH):
        x = layer_norm(ALPHA * x + 0.5 * swiglu_2(x, ffn1_w13[l], ffn1_w2[l]), ln_g[l, 0], ln_b[l, 0])
        m = mixer(x, w_in[l], lower_bounds[l], hg_norm_g[l], sg_ln_g[l], sg_ln_b[l], sg_ws[l],
                  sg_bs[l], w_branch_a[l], w_branch_b[l], w_out[l])
        x = layer_norm(ALPHA * x + m, ln_g[l, 1], ln_b[l, 1])
        x = layer_norm(ALPHA * x + 0.5 * swiglu_2(x, ffn2_w13[l], ffn2_w2[l]), ln_g[l, 2], ln_b[l, 2])
    return x


def setup_inputs(seed=0):
    out = dict(first_inputs(seed))
    for name, value in second_inputs(seed + 1).items():
        if name != "x":
            out[name + "_2"] = value
    return out


def reference(
    x, c, ctx, c_ctx, ada_w, ada_b, norm1_g, norm2_g, w_in, conv_w, conv_b, cnorm_g, cnorm_b,
    shift_w, decay_b0, decay_up, iclr_b0, iclr_up, k_k, k_a, g_up, r_k, gn_g, gn_b, w_out,
    ffn_wg, ffn_wu, ffn_wd, final_g, ffn1_w13_2, ffn1_w2_2, ffn2_w13_2, ffn2_w2_2, ln_g_2,
    ln_b_2, w_in_2, hg_lb_2, hg_norm_g_2, sg_ln_g_2, sg_ln_b_2, sg_ws_2, sg_bs_2, w_branch_a_2,
    w_branch_b_2, w_out_2,
):
    x = first_block(
        x, c, ctx, c_ctx, ada_w, ada_b, norm1_g, norm2_g, w_in, conv_w, conv_b, cnorm_g,
        cnorm_b, shift_w, decay_b0, decay_up, iclr_b0, iclr_up, k_k, k_a, g_up, r_k, gn_g, gn_b,
        w_out, ffn_wg, ffn_wu, ffn_wd, final_g,
    )
    return second_block(
        x, ffn1_w13_2, ffn1_w2_2, ffn2_w13_2, ffn2_w2_2, ln_g_2, ln_b_2, w_in_2, hg_lb_2,
        hg_norm_g_2, sg_ln_g_2, sg_ln_b_2, sg_ws_2, sg_bs_2, w_branch_a_2, w_branch_b_2,
        w_out_2,
    )


_drawn_inputs = setup_inputs


def setup_inputs(seed=0):
    import zlib

    import numpy as np

    out = dict(_drawn_inputs(seed))
    spreads = {}
    factors = {'norm1_g': 4.981,
     'norm2_g': 6.427,
     'conv_b': 32.44,
     'cnorm_g': 64.0,
     'cnorm_b': 64.0,
     'decay_up': 6.679,
     'k_k': 28.784,
     'k_a': 8.789,
     'gn_g': 64.0,
     'gn_b': 64.0,
     'hg_norm_g_2': 36.024,
     'sg_ln_g_2': 49.084,
     'sg_ln_b_2': 43.257,
     'sg_bs_2': 6.201}
    for name, (base, spread) in spreads.items():
        noise = np.random.default_rng([zlib.crc32(name.encode()), seed]).standard_normal(out[name].shape)
        drawn = base * np.exp(spread * noise) if base else spread * noise
        out[name] = __import__('jax').numpy.asarray(drawn.astype(out[name].dtype))
    for name, factor in factors.items():
        out[name] = (out[name] * factor).astype(out[name].dtype)
    return out
```

```python
from contextlib import ExitStack

import concourse.bass as bass
import numpy as np
from concourse import mybir
from concourse.alu_op_type import AluOpType as ALU

F32 = mybir.dt.float32
ACT = mybir.ActivationFunctionType

P = 128
D = 1024
KD = D // P
T = 256
FF = 2816
KF = FF // P
DEPTH = 2
CONV_K = 31
PAD = CONV_K // 2
ZW = T + 2 * PAD
RMS_EPS, LN_EPS, GN_EPS = 1e-6, 1e-5, 64e-5
KAPPA = 0.606531
ALPHA = (2 * DEPTH) ** 0.25
C = 64
NCH = 2 * T // C
LEVELS = 6
RING = 4
SLOT = 11 * P
SLABS2 = 2 * (2 * KF + 16) + 40 + 8 + 8
HB = 16
NB = T // HB
HH = 4

CONSTS = [("ident", P), ("ones", P), ("blk64", P), ("cum", 4 * P), ("m1", 2 * P), ("inv", 2 * LEVELS * C),
          ("neg0", 4 * C), ("eye64", C), ("tril", P), ("pick", 2)]
PARAMS1 = [("n1g", 8), ("n2g", 8), ("cw", 4 * CONV_K), ("cb", 4), ("cng", 4), ("cnb", 4), ("sw", 15 * 3),
           ("db0", 0), ("ib0", 8), ("kk", 4), ("ka", 4), ("rk", 4), ("gng", 4), ("gnb", 4), ("adab", 48)]
PARAMS2 = [("lng", 24), ("lnb", 24), ("ng", 4), ("slg", 4), ("slb", 4)]


def columns(table):
    at, out = 0, {}
    for name, n in table:
        out[name] = at
        at += n
    return out, at


CCOL, CN = columns(CONSTS)
PCOL, PN = columns(PARAMS1)
QCOL, QN = columns(PARAMS2)


def build(nc, a, out):
    ctx = ExitStack()
    sem_names = ["slab_used", "bank_full", "free_dve", "free_act", "act_ready", "pe_phase", "act_phase",
                 "dve_phase", "pool_phase", "pe_step", "act_step", "dve_step", "pool_step",
                 "consts_in", "layer_in", "x_in", "store",
                 "ada_full", "ada_copied"]
    settled_names = [n + "_settled" for n in ("pe", "act", "dve", "pool")]
    with ctx:
        S = {n: ctx.enter_context(nc.semaphore(n)) for n in sem_names + settled_names}
        slab_loaded = [ctx.enter_context(nc.semaphore(f"slab_loaded{i}")) for i in range(RING)]
        wk = {n: [ctx.enter_context(nc.semaphore(f"wkv_{n}{d}")) for d in range(2)]
              for n in ("pe", "act", "dve", "pool")}
        arena = ctx.enter_context(nc.sbuf_tensor("arena", [P, 53200], F32))
        bank = [ctx.enter_context(nc.psum_tensor(f"bank{i}", [P, 512], F32)) for i in range(8)]

        def view(at, *dims):
            n = int(np.prod(dims))
            assert at + n <= 53200
            v = arena[:, at:at + n]
            if len(dims) == 1:
                return v
            names = "abcd"[:len(dims)]
            pat = "p (" + " ".join(names) + ") -> p " + " ".join(names)
            return v.rearrange(pat, **{k: d for k, d in zip(names[1:], dims[1:])})

        X0, H0, R0, U0 = 0, 4096, 8192, 24576
        M0, G0 = U0 + 15 * 512, U0 + 15 * 512 + 4096
        C0 = G0 + RING * SLOT
        K0 = C0 + CN
        K1 = K0 + 2 * PN + 8 + 2 * QN + 8
        MOD0 = K1
        SM0 = MOD0 + 2 * 96 + 64 + 16
        CH0 = SM0 + 192
        X = view(X0, KD, 2, T)
        H = view(H0, KD, 2, T)
        cst = arena[:, C0:C0 + CN]

        def con(name, *dims):
            return view(C0 + CCOL[name], *dims)

        ident, ones, blk64 = con("ident", P), con("ones", P), con("blk64", P)
        cum = con("cum", 2, 2, P)
        m1 = con("m1", 2, P)
        inv = con("inv", 2, LEVELS, C)
        neg0 = con("neg0", 2, 2, C)
        eye64 = con("eye64", C)
        tril = con("tril", P)
        pick = con("pick", 2)

        def par(l, name, *dims):
            return view(K0 + l * PN + PCOL[name], *dims)

        final_g = view(K0 + 2 * PN, 8)
        P2 = K0 + 2 * PN + 8

        def par2(name, n):
            return arena[:, P2:P2 + 2 * QN].rearrange("p (l n) -> p l n", l=2)[:, :, QCOL[name]:QCOL[name] + n]

        hg_lb = view(P2 + 2 * QN, 2, 4)
        MOD = [view(MOD0 + 96 * l, 48, 2) for l in range(2)]
        GS = [view(MOD0 + 192 + 16 * n, KD, 2) for n in range(4)]
        cond = view(MOD0 + 256, KD, 2)
        FS = view(SM0, 2, 4, NCH)
        DM = view(SM0 + 64, 2, 4, NCH)
        DE = view(SM0 + 128, 2, 4, NCH)

        class Eng:

            def __init__(self, eng, name):
                self.e, self.name = eng, name
                self.c = {n: 0 for n in sem_names}
                self.wk = 0
                self.slab = 0
                self.l = None

            def v(self, name, n):
                x = self.c[name] + n
                return x if self.l is None else x + self.l * PER[name]

        def settled(E):
            E.e.sem_inc(S[E.name + "_settled"], 1)

        def phase(E):
            E.e.drain().then_inc(S[E.name + "_phase"], 1)
            for o in ("pe", "act", "dve", "pool"):
                E.c[o + "_phase"] += 1
                if o != E.name:
                    E.e.wait_ge(S[o + "_phase"], E.v(o + "_phase", 0))
            if E.l is not None:
                settled(E)

        def repeat(E, n, body, fn):
            if n // body > 1:
                with E.e.Fori(0, n // body) as i:
                    fn(i, body)
            elif n // body == 1:
                fn(0, body)
            if n % body:
                fn(n // body, n % body)

        def slab_to_slot(E, s, i, body, src, w):
            k = E.slab + s
            n = i * body + (k + 1)
            E.e.wait_ge(S["slab_used"], n if E.l is None else E.l * SLABS2 + n)
            slot = (k if not isinstance(i, int) else k + i * body) % RING
            E.e.dma_start(view(G0 + slot * SLOT, w), src).then_inc(slab_loaded[slot], 16)

        def load_slabs(E, src, n, tiles, body=4, first=0):
            w = tiles * P

            def some(i, count):
                for s in range(count):
                    slab_to_slot(E, s, i, body, src(i * body + s + first), w)

            repeat(E, n, body, some)
            E.slab += n

        def slab_wait(E, s, i, body):
            k = E.slab + s
            val = 16 * (k // RING + 1)
            if not isinstance(i, int):
                val = i * (16 * body // RING) + val
            else:
                val = 16 * ((k + i * body) // RING + 1)
            if E.l is not None:
                val = E.l * (16 * SLABS2 // RING) + val
            slot = (k if not isinstance(i, int) else k + i * body) % RING
            E.e.wait_ge(slab_loaded[slot], val)
            return view(G0 + slot * SLOT, 11, P)

        def gemm_pe(E, units, K, tiles, rhs, N, free, body=4):
            per = body * K // tiles
            assert units <= body or (per % RING == 0 and body % 4 == 0 and body * K % tiles == 0)

            def some(i, count):
                t = 0
                for u in range(count):
                    E.e.wait_ge(S[free], E.v(free, i * body + u + 1))
                    for k in range(K):
                        if t % tiles == 0:
                            w = slab_wait(E, t // tiles, i, per)
                        mm = E.e.matmul(bank[u % 4][:, 0:N], w[:, t % tiles, :], rhs(k), start=(k == 0), stop=(k == K - 1))
                        if t % tiles == 0:
                            mm.then_inc(S["slab_used"], 1)
                        t += 1
                    mm.then_inc(S["bank_full"], 1)

            repeat(E, units, body, some)
            E.slab += units * K // tiles

        def units_done(E, n, free, pairs=0):
            E.c["bank_full"] += n
            E.c[free] += n
            E.c["act_ready"] += pairs

        def gated_act(E, n, func, N, tmp):
            def some(i, count):
                for q in range(count // 2):
                    E.e.wait_ge(S["bank_full"], E.v("bank_full", i * 4 + 2 * q + 1))
                    E.e.wait_ge(S["free_dve"], E.v("free_dve", i * 4 + 2 * q + 2))
                    E.e.activation(tmp[:, q % 2, 0:N], bank[2 * q][:, 0:N], func).then_inc(S["act_ready"], 1)
            repeat(E, n, 4, some)

        def gated_dve(E, n, dst, N, tmp):
            def some(i, count):
                for q in range(count // 2):
                    E.e.wait_ge(S["act_ready"], E.v("act_ready", i * 2 + q + 1))
                    E.e.wait_ge(S["bank_full"], E.v("bank_full", i * 4 + 2 * q + 2))
                    E.e.tensor_tensor(dst(i * 2 + q), tmp[:, q % 2, 0:N], bank[2 * q + 1][:, 0:N],
                                      ALU.mult).then_inc(S["free_dve"], 2)
            repeat(E, n, 4, some)

        def take_units(E, free, n, fn, body=4):
            def some(i, count):
                for u in range(count):
                    E.e.wait_ge(S["bank_full"], E.v("bank_full", i * body + u + 1))
                    fn(i * body + u, bank[u % 4]).then_inc(S[free], 1)
            repeat(E, n, body, some)

        def steps(E, pe=0, act=0, dve=0, pool=0):
            for k, n in (("pe", pe), ("act", act), ("dve", dve), ("pool", pool)):
                E.c[k + "_step"] += n

        def one(n):
            return slice(n, n + 1) if isinstance(n, int) else bass.ds(n, 1)

        def cols(at, n):
            return slice(at, at + n) if isinstance(at, int) else bass.ds(at, n)

        XF = view(X0, KD, 2 * T)
        HF = view(H0, KD, 2 * T)
        MIXF = view(M0, KD, 2 * T)

        def rstd_dve(E, pairs, inv_n, eps):
            for src, dst in pairs:
                E.e.tensor_scalar(dst, src, inv_n, eps, ALU.mult, ALU.add)
            E.e.drain()
            for src, dst in pairs:
                E.e.reciprocal(dst, dst).then_inc(S["dve_step"], 1)

        def rms(E, N, gs, shift, dst):
            rs = view(CH0, 2 * T)
            if E.name == "act":
                for k in range(KD):
                    E.e.activation(HF[:, k, 0:N], XF[:, k, 0:N], ACT.Square).then_inc(S["act_step"], 1)
                E.e.wait_ge(S["dve_step"], E.v("dve_step", 1))
                E.e.activation(rs[:, 0:N], rs[:, 0:N], ACT.Sqrt).then_inc(S["act_step"], 1)
                if shift is not None:
                    for k in range(KD):
                        E.e.wait_ge(S["dve_step"], E.v("dve_step", 2 + k))
                        for s in range(N // T):
                            E.e.activation(dst[:, k, s * T:(s + 1) * T], dst[:, k, s * T:(s + 1) * T], ACT.Identity, bias=shift(k, s))
            if E.name == "pe":
                for k in range(KD):
                    E.e.wait_ge(S["act_step"], E.v("act_step", k + 1))
                    mm = E.e.matmul(bank[4][:, 0:N], ones, HF[:, k, 0:N], start=(k == 0), stop=(k == KD - 1))
                mm.then_inc(S["pe_step"], 1)
            if E.name == "dve":
                E.e.wait_ge(S["pe_step"], E.v("pe_step", 1))
                rstd_dve(E, [(bank[4][:, 0:N], rs[:, 0:N])], 1.0 / D, RMS_EPS)
                E.e.wait_ge(S["act_step"], E.v("act_step", KD + 1))
                for k in range(KD):
                    for s in range(N // T):
                        ins = E.e.scalar_tensor_tensor(out=dst[:, k, s * T:(s + 1) * T], in0=XF[:, k, s * T:(s + 1) * T],
                                                       scalar=gs(k, s), in1=rs[:, s * T:(s + 1) * T],
                                                       op0=ALU.mult, op1=ALU.mult)
                    ins.then_inc(S["dve_step"], 1)
            steps(E, pe=1, act=KD + 1, dve=1 + KD)
            phase(E)

        def layer_norm(E, src, dst, K, gain, shift, scr):
            cen, sq, rs = view(scr, K, T), view(scr + K * T, K, T), view(scr + 2 * K * T, T)
            if E.name == "pe":
                for k in range(K):
                    mm = E.e.matmul(bank[4][:, 0:T], ones, src(k), start=(k == 0), stop=(k == K - 1))
                mm.then_inc(S["pe_step"], 1)
                for k in range(K):
                    E.e.wait_ge(S["act_step"], E.v("act_step", k + 1))
                    mm = E.e.matmul(bank[5][:, 0:T], ones, sq[:, k, :], start=(k == 0), stop=(k == K - 1))
                mm.then_inc(S["pe_step"], 1)
            if E.name == "dve":
                E.e.wait_ge(S["pe_step"], E.v("pe_step", 1))
                for k in range(K):
                    E.e.scalar_tensor_tensor(out=cen[:, k, :], in0=bank[4][:, 0:T], scalar=-1.0 / (K * P),
                                                     in1=src(k), op0=ALU.mult, op1=ALU.add).then_inc(S["dve_step"], 1)
                E.e.wait_ge(S["pe_step"], E.v("pe_step", 2))
                rstd_dve(E, [(bank[5][:, 0:T], rs)], 1.0 / (K * P), LN_EPS)
                E.e.wait_ge(S["act_step"], E.v("act_step", K + 1))
                for k in range(K):
                    E.e.scalar_tensor_tensor(out=dst(k), in0=cen[:, k, :], scalar=gain(k), in1=rs,
                                                     op0=ALU.mult, op1=ALU.mult).then_inc(S["dve_step"], 1)
            if E.name == "act":
                for k in range(K):
                    E.e.wait_ge(S["dve_step"], E.v("dve_step", k + 1))
                    E.e.activation(sq[:, k, :], cen[:, k, :], ACT.Square).then_inc(S["act_step"], 1)
                E.e.wait_ge(S["dve_step"], E.v("dve_step", K + 1))
                E.e.activation(rs, rs, ACT.Sqrt).then_inc(S["act_step"], 1)
                for k in range(K):
                    E.e.wait_ge(S["dve_step"], E.v("dve_step", K + 2 + k))
                    E.e.activation(dst(k), dst(k), ACT.Identity, bias=shift(k))
            steps(E, pe=2, act=K + 1, dve=2 * K + 1)
            phase(E)

        def head_norm(E, src, N, eps, scr):
            cen, sq = view(scr, 4, N), view(scr + 4 * N, 4, N)
            if E.name == "pe":
                for k in range(4):
                    E.e.matmul(bank[4 + k][:, 0:N], blk64, src(k), start=True, stop=True).then_inc(S["pe_step"], 1)
                for k in range(4):
                    E.e.wait_ge(S["act_step"], E.v("act_step", k + 1))
                    E.e.matmul(bank[k][:, 0:N], blk64, sq[:, k, :], start=True, stop=True).then_inc(S["pe_step"], 1)
            if E.name == "dve":
                for k in range(4):
                    E.e.wait_ge(S["pe_step"], E.v("pe_step", k + 1))
                    E.e.scalar_tensor_tensor(out=cen[:, k, :], in0=bank[4 + k][:, 0:N], scalar=-1.0 / C,
                                                     in1=src(k), op0=ALU.mult, op1=ALU.add).then_inc(S["dve_step"], 1)
                E.e.wait_ge(S["pe_step"], E.v("pe_step", 8))
                rstd_dve(E, [(bank[k][:, 0:N], sq[:, k, :]) for k in range(4)], 1.0 / C, eps)
                for k in range(4):
                    E.e.wait_ge(S["act_step"], E.v("act_step", 5 + k))
                    E.e.tensor_tensor(cen[:, k, :], cen[:, k, :], sq[:, k, :], ALU.mult)
            if E.name == "act":
                for k in range(4):
                    E.e.wait_ge(S["dve_step"], E.v("dve_step", k + 1))
                    E.e.activation(sq[:, k, :], cen[:, k, :], ACT.Square).then_inc(S["act_step"], 1)
                for k in range(4):
                    E.e.wait_ge(S["dve_step"], E.v("dve_step", 5 + k))
                    E.e.activation(sq[:, k, :], sq[:, k, :], ACT.Sqrt).then_inc(S["act_step"], 1)
            steps(E, pe=8, act=8, dve=8)
            phase(E)

        def column_major(ap):
            return ap.rearrange("p (r c) -> p c r", r=4)

        def by_four(ap):
            return ap.rearrange("p (c r) -> p c r", r=4)

        US = view(U0, 15, 2 * T)
        Z = view(R0, 4, 2, ZW)
        QK = view(R0, 8, 2, 2 * T)
        KB = view(R0 + 8192, 8, 2, 2 * T)
        ADA_FIRST = 27

        silu_c = view(CH0 + 2560, KD, 32)
        ada_rows = view(CH0 + 2816, 2, 3 * P)

        def ada_sums(E, u, s, i, per):
            for q in range(3):
                w = slab_wait(E, s + q, i, per)
                for k in range(KD):
                    r = 32 * (k % 4)
                    mm = E.e.matmul(bank[5 + u % 2][r:r + 32, q * P:(q + 1) * P], silu_c[:, k, :], w[:, k, :],
                                    start=(k < 4), stop=(k >= 4), skip_group_check=True)
                    if k == 0:
                        mm.then_inc(S["slab_used"], 1)
            mm.then_inc(S["ada_full"], 1)

        def ada_turn(E, u, n, chunk):
            E.e.wait_ge(S["ada_copied"], E.v("ada_copied", n + 1))
            for q in range(3):
                E.e.matmul(bank[7][:, cols((chunk + q) * 2, 2)], ada_rows[:, u % 2, q * P:(q + 1) * P], pick,
                           start=True, stop=True)

        def ada_copy(E, u, n):
            E.e.wait_ge(S["ada_full"], E.v("ada_full", n + 1))
            E.e.activation(ada_rows[:, u % 2, :], bank[5 + u % 2][:, 0:3 * P], ACT.Copy).then_inc(S["ada_copied"], 1)

        def trios_done(E, n):
            E.c["ada_full"] += n
            E.c["ada_copied"] += n

        def modulation_start(E):
            if E.name == "dve":
                E.e.memset(silu_c, 0.0).then_inc(S["dve_step"], 1)
            if E.name == "act":
                E.e.wait_ge(S["dve_step"], E.v("dve_step", 1))
                E.e.activation(silu_c[:, :, 0:2], cond, ACT.Silu).then_inc(S["act_step"], 1)

                def some(i, count):
                    for u in range(count):
                        ada_copy(E, u, i * 4 + u)
                repeat(E, ADA_FIRST // 3, 4, some)
            if E.name == "pe":
                E.e.wait_ge(S["act_step"], E.v("act_step", 1))

                def some(i, count):
                    for u in range(count):
                        ada_sums(E, u, 3 * u, i, 12)
                        if u:
                            ada_turn(E, u - 1, i * 4 + (u - 1), i * 12 + 3 * (u - 1))
                    ada_turn(E, count - 1, i * 4 + (count - 1), i * 12 + 3 * (count - 1))
                repeat(E, ADA_FIRST // 3, 4, some)
                E.slab += ADA_FIRST
            steps(E, act=1, dve=1)
            trios_done(E, ADA_FIRST // 3)
            phase(E)
            if E.name == "dve":
                modulation_out(E, 0, 0, 16)
                norm_gain(E, 0, 0)
            phase(E)

        def modulation_out(E, l, m0, m1_):
            b = bank[7][:, 96 * l + 2 * m0:96 * l + 2 * m1_].rearrange("p (m s) -> p m s", s=2)
            E.e.tensor_tensor(MOD[l][:, m0:m1_, :], b,
                              par(l, "adab", 48, 1)[:, m0:m1_, :].broadcast_to([P, m1_ - m0, 2]), ALU.add)
            E.e.drain()

        def norm_gain(E, l, n):
            g = GS[2 * l + n]
            E.e.tensor_scalar(g, MOD[l][:, 24 * n + 8:24 * n + 16, :], 1.0, None, ALU.add)
            E.e.drain()
            E.e.tensor_tensor(g, g, par(l, "n1g" if n == 0 else "n2g", 8, 1).broadcast_to([P, 8, 2]), ALU.mult)

        def input_projection(E, l):
            Nc = 2 * T if l == 0 else T
            S_ = Nc // T
            side = 3 if l == 0 else 0
            tmp = view(CH0, 2, 512)
            raw = view(CH0 + 1024, 2, 2, T + 2)
            if E.name == "pe":
                for units, N, chunk0 in ((8, Nc, ADA_FIRST), (15, 2 * T, ADA_FIRST + 24)):
                    per = 4 * (1 + side)

                    def turn(i, u):
                        ada_turn(E, u, i * 4 + u, i * 12 + (chunk0 + 3 * u))

                    def some(i, count):
                        for u in range(count):
                            E.e.wait_ge(S["free_dve"], E.v("free_dve", i * 4 + u + 1))
                            w = slab_wait(E, u * (1 + side), i, per)
                            for k in range(KD):
                                mm = E.e.matmul(bank[u % 4][:, 0:N], w[:, k, :], HF[:, k, 0:N],
                                                start=(k == 0), stop=(k == KD - 1))
                                if k == 0:
                                    mm.then_inc(S["slab_used"], 1)
                            mm.then_inc(S["bank_full"], 1)
                            if side:
                                if u:
                                    turn(i, u - 1)
                                ada_sums(E, u, 4 * u + 1, i, per)
                        if side:
                            turn(i, count - 1)
                    repeat(E, units, 4, some)
                    E.slab += units * (1 + side)
                    units_done(E, units, "free_dve")
                    if side:
                        trios_done(E, units)
            else:
                if E.name == "act":
                    def some(i, count):
                        for q in range(2):
                            E.e.wait_ge(S["bank_full"], E.v("bank_full", i * 4 + 2 * q + 1))
                            E.e.wait_ge(S["free_dve"], E.v("free_dve", i * 4 + 2 * q + 2))
                            E.e.activation(tmp[:, q % 2, 0:Nc], bank[2 * q][:, 0:Nc], ACT.Sigmoid).then_inc(S["act_ready"], 1)
                            if side:
                                ada_copy(E, 2 * q, i * 4 + 2 * q)
                                ada_copy(E, 2 * q + 1, i * 4 + (2 * q + 1))
                    repeat(E, 8, 4, some)
                if E.name == "dve":
                    E.e.memset(Z, 0.0)
                    E.e.memset(raw, 0.0)
                    E.e.drain()

                    def some(i, count):
                        for q in range(2):
                            E.e.wait_ge(S["act_ready"], E.v("act_ready", i * 2 + q + 1))
                            E.e.wait_ge(S["bank_full"], E.v("bank_full", i * 4 + 2 * q + 2))
                            for s in range(S_):
                                o = Z[:, one(i * 2 + q), s, PAD:PAD + T].rearrange("p o t -> p (o t)")
                                i0, i1 = tmp[:, q, s * T:(s + 1) * T], bank[2 * q + 1][:, s * T:(s + 1) * T]
                                if l == 1:
                                    o, i0, i1 = by_four(o), column_major(i0), column_major(i1)
                                ins = E.e.tensor_tensor(o, i0, i1, ALU.mult)
                            ins.then_inc(S["free_dve"], 2)
                    repeat(E, 8, 4, some)
                    E.e.drain()
                units_done(E, 8, "free_dve", 4)
                if side:
                    trios_done(E, 8)
                if E.name == "act":
                    def some(i, count):
                        for u in range(count):
                            E.e.wait_ge(S["bank_full"], E.v("bank_full", i * 4 + u + 1))
                            E.e.wait_ge(S["free_dve"], E.v("free_dve", i * 4 + u + 3))
                            src = bank[u % 4][:, :].rearrange("p (s t) -> p s t", t=T)
                            if l == 0:
                                ins = E.e.activation(raw[:, u % 2, :, 1:T + 1], src, ACT.Copy)
                            else:
                                E.e.activation(by_four(raw[:, u % 2, 0, 1:T + 1]), column_major(src[:, 0, :]), ACT.Copy)
                                ins = E.e.activation(raw[:, u % 2, 1, 1:T + 1], src[:, 1, :], ACT.Copy)
                            ins.then_inc(S["act_ready"], 1)
                            if side:
                                ada_copy(E, u, i * 4 + u)
                    repeat(E, 15, 4, some)
                if E.name == "dve":
                    sw, cw, cb = par(l, "sw", 15, 3), par(l, "cw", 4, CONV_K), par(l, "cb", 4)

                    def wide(t, first=False):
                        for k in range(4):
                            o = MIXF[:, k, 0:Nc].rearrange("p (s t) -> p s t", t=T)
                            z = Z[:, k, 0:S_, cols(t, T)]
                            if first:
                                E.e.tensor_scalar(o, z, cw[:, k, 0:1], cb[:, k:k + 1], ALU.mult, ALU.add)
                            else:
                                E.e.scalar_tensor_tensor(out=o, in0=z, scalar=cw[:, k, one(t)], in1=o,
                                                         op0=ALU.mult, op1=ALU.add)
                        E.e.drain()

                    wide(0, True)

                    def some(i, count):
                        for u in range(count):
                            n = i * 2 + u
                            E.e.wait_ge(S["act_ready"], E.v("act_ready", n + 1))
                            o = US[:, one(n), :].rearrange("p o (s t) -> p (o s) t", t=T)
                            E.e.tensor_scalar(o, raw[:, u, :, 1:T + 1], sw[:, one(n), 1], None, ALU.mult)
                            for tap in (0, 2):
                                E.e.drain()
                                ins = E.e.scalar_tensor_tensor(out=o, in0=raw[:, u, :, tap:tap + T],
                                                               scalar=sw[:, one(n), tap], in1=o, op0=ALU.mult, op1=ALU.add)
                            ins.then_inc(S["free_dve"], 1)
                            wide(n * 2 + 1)
                            wide(n * 2 + 2)
                    repeat(E, 15, 2, some)
                units_done(E, 15, "free_dve", 15)
                if side:
                    trios_done(E, 15)
            if E.name == "pe":
                E.c["act_ready"] += 19
            phase(E)

        SIG = view(H0, 8, 512)
        DU, IU = view(M0 + 2048, 1024), view(M0 + 3072, 1024)
        GU = view(CH0, 2, 512)
        WL = view(CH0 + 1024, 512)
        KKN = view(CH0 + 1536, 4, 512)
        NR = view(CH0 + 3584, 4, 512)
        AR = view(CH0 + 5632, 2, 512)
        EN = view(CH0 + 6656, 2, 512)

        def rwkv_prep(E, l):
            if E.name == "act":
                for dst, src in ((DU[0:65, :], a["decay_w"][l]), (IU[64:128, :], a["iclr_w"][l]), (GU, a["gate_w"][l])):
                    E.e.dma_start(dst, src).then_inc(S["layer_in"], 16)
                E.e.activation(WL[0:64, :], US[0:64, 12, :], ACT.Tanh).then_inc(S["act_step"], 1)
                E.e.activation(US[:, 13, :], US[:, 13, :], ACT.Sigmoid)
                E.e.activation(US[0:32, 14, :], US[0:32, 14, :], ACT.Sigmoid)
            if E.name == "pool":
                for p in range(4):
                    E.e.tensor_scalar(KKN[:, p, :], US[:, 4 + p, :], par(l, "kk", 4)[:, p:p + 1], None, ALU.mult)
                E.e.drain()
                for p in range(4):
                    E.e.tensor_tensor(NR[:, p, :], KKN[:, p, :], KKN[:, p, :], ALU.mult)
            if E.name == "dve":
                E.e.memset(WL[64:65, :], 1.0)
            if E.name == "dve" and l == 0:
                modulation_out(E, 0, 16, 48)
                modulation_out(E, 1, 0, 48)
                for n in ((0, 1), (1, 0), (1, 1)):
                    norm_gain(E, *n)
            E.c["layer_in"] += 48
            steps(E, act=1)
            phase(E)
            if E.name == "pe":
                for p in range(4):
                    E.e.matmul(bank[p][:, :], blk64, NR[:, p, :], start=True, stop=True).then_inc(S["pe_step"], 1)
            if E.name == "act":
                for p in range(4):
                    E.e.wait_ge(S["pe_step"], E.v("pe_step", p + 1))
                    E.e.activation(NR[:, p, :], bank[p][:, :], ACT.Sqrt).then_inc(S["act_step"], 1)
            if E.name == "dve":
                E.e.wait_ge(S["act_step"], E.v("act_step", 4))
                for op in ("max", "inv", "mul"):
                    for p in range(4):
                        if op == "max":
                            E.e.tensor_scalar(NR[:, p, :], NR[:, p, :], 1e-12, None, ALU.max)
                        elif op == "inv":
                            E.e.reciprocal(NR[:, p, :], NR[:, p, :])
                        else:
                            E.e.tensor_tensor(KKN[:, p, :], KKN[:, p, :], NR[:, p, :], ALU.mult)
                    E.e.drain()
            steps(E, pe=4, act=4)
            phase(E)
            if E.name == "pe":
                E.e.wait_ge(S["layer_in"], E.v("layer_in", 0))
                for g in range(8):
                    d, j = divmod(g, 4)
                    E.e.matmul(bank[g][:, :], WL[0:65, j * P:(j + 1) * P], DU[0:65, d * 512:(d + 1) * 512],
                                       start=True, stop=True).then_inc(S["pe_step"], 1)
                for g in range(8):
                    d, p = divmod(g, 4)
                    E.e.wait_ge(S["act_step"], E.v("act_step", 8 if g < 2 else 8 + g - 1))
                    for x in range(2):
                        for j in range(4):
                            E.e.matmul(bank[2 * (g % 2) + x][:, j * P:(j + 1) * P], SIG[:, d * 4 + j, p * P:(p + 1) * P],
                                       cum[:, d, x, :], start=True, stop=True)
                    E.e.matmul(bank[4 + g % 2][:, :], IU[64:128, d * 512 + p * P:d * 512 + (p + 1) * P],
                                       US[64:128, 12, :], start=True, stop=True).then_inc(S["pe_step"], 1)
            if E.name == "act":
                for g in range(8):
                    E.e.wait_ge(S["pe_step"], E.v("pe_step", g + 1))
                    E.e.activation(SIG[:, g, :], bank[g][:, :], ACT.Sigmoid).then_inc(S["act_step"], 1)
                for g in range(8):
                    d, p = divmod(g, 4)
                    E.e.wait_ge(S["pe_step"], E.v("pe_step", 9 + g))
                    if g >= 2:
                        E.e.wait_ge(S["dve_step"], E.v("dve_step", g - 1))
                    A, B = bank[2 * (g % 2)][:, :], bank[2 * (g % 2) + 1][:, :]
                    first, last = (0, C - 1) if d == 0 else (C - 1, 0)
                    E.e.activation(AR[:, g % 2, :], bank[4 + g % 2][:, :], ACT.Sigmoid, bias=par(l, "ib0", 8)[:, g:g + 1])
                    E.e.activation(QK[:, g, 1, :], A, ACT.Exp, scale=-KAPPA)
                    E.e.activation(EN[:, g % 2, :], A, ACT.Exp, scale=KAPPA)
                    E.e.activation(QK[:, g, 0, :], B, ACT.Exp, scale=-KAPPA)
                    E.e.activation(DE[:, d, p, :], A[:, last::C], ACT.Exp, scale=-KAPPA)
                    E.e.activation(DM[:, d, p, :], B[:, first::C], ACT.Exp, scale=KAPPA).then_inc(S["act_step"], 1)
            if E.name == "pool":
                for g in range(8):
                    E.e.wait_ge(S["act_step"], E.v("act_step", 9 + g))
                    E.e.tensor_tensor(QK[:, g, 1, :], QK[:, g, 1, :], US[:, g % 4, :], ALU.mult)
                    E.e.tensor_tensor(QK[:, g, 0, :], QK[:, g, 0, :], KKN[:, g % 4, :], ALU.mult)
            if E.name == "dve":
                ka = par(l, "ka", 4)
                for g in range(8):
                    p = g % 4
                    E.e.wait_ge(S["act_step"], E.v("act_step", 9 + g))
                    kd = NR[:, g % 2, :]
                    ar, en = AR[:, g % 2, :], EN[:, g % 2, :]
                    E.e.tensor_scalar(kd, ar, -1.0, ka[:, p:p + 1], ALU.add, ALU.mult)
                    E.e.drain()
                    E.e.scalar_tensor_tensor(out=kd, in0=kd, scalar=1.0, in1=US[:, 4 + p, :], op0=ALU.add, op1=ALU.mult)
                    E.e.tensor_tensor(ar, ar, KKN[:, p, :], ALU.mult)
                    E.e.drain()
                    E.e.tensor_tensor(KB[:, g, 0, :], kd, en, ALU.mult)
                    E.e.tensor_tensor(KB[:, g, 1, :], ar, en, ALU.mult).then_inc(S["dve_step"], 1)
            steps(E, pe=16, act=16, dve=8)
            phase(E)
            if E.name == "dve":
                for f0, c0, c1, n in ((0, 4, 5, 3), (3, 7, 0, 1), (4, 0, 1, 3)):
                    E.e.tensor_tensor(FS[:, 0, :, f0:f0 + n], DE[:, 0, :, c0:c0 + n], DM[:, 0, :, c1:c1 + n], ALU.mult)
                E.e.tensor_tensor(FS[:, 1, :, 1:8], DE[:, 1, :, 1:8], DM[:, 1, :, 0:7], ALU.mult)
                E.e.memset(FS[:, 0, :, 7:8], 1.0)
                E.e.memset(FS[:, 1, :, 0:1], 1.0)
                for p in range(4):
                    E.e.scalar_tensor_tensor(out=NR[:, p, :], in0=US[:, p, :], scalar=par(l, "rk", 4)[:, p:p + 1],
                                                     in1=US[:, 4 + p, :], op0=ALU.mult, op1=ALU.mult).then_inc(S["dve_step"], 1)
                for p in range(4):
                    E.e.wait_ge(S["pe_step"], E.v("pe_step", 2 * p + 1))
                    E.e.tensor_tensor(US[:, p, :], bank[p][:, :], US[:, 8 + p, :], ALU.mult)
            if E.name == "pe":
                for p in range(4):
                    E.e.wait_ge(S["dve_step"], E.v("dve_step", p + 1))
                    E.e.matmul(bank[p][:, :], blk64, NR[:, p, :], start=True, stop=True).then_inc(S["pe_step"], 1)
                    E.e.matmul(bank[4 + p][:, :], GU[:, 0, p * P:(p + 1) * P], US[:, 13, :], start=True, stop=False)
                    E.e.matmul(bank[4 + p][:, :], GU[0:32, 1, p * P:(p + 1) * P], US[0:32, 14, :], start=False, stop=True).then_inc(S["pe_step"], 1)
            if E.name == "act":
                for p in range(4):
                    E.e.wait_ge(S["pe_step"], E.v("pe_step", 2 * p + 2))
                    E.e.activation(US[:, 4 + p, :], bank[4 + p][:, :], ACT.Copy)
            steps(E, pe=8, dve=4)
            phase(E)

        def both(at, *dims):
            n = int(np.prod(dims))
            return [view(at + d * n, *dims) for d in range(2)]

        Gm = both(H0 + 2048, 2, 4, P)
        LB = both(U0 + 12 * 512, 4, 2, C)
        AM = [view(U0 + 14 * 512, 2, 4, C), view(CH0, 2, 4, C)]
        QC = both(CH0 + 512, 4, 2, C)
        VC = both(CH0 + 1536, 4, C)
        LT = both(CH0 + 2048, 4, P)
        UV = both(CH0 + 3072, 4, 2, C)
        AN = both(CH0 + 4096, 2, 4, C)
        TN = both(CH0 + 5120, 2, 4, C)
        P1 = both(CH0 + 6144, 4, C)
        XN = both(CH0 + 6656, 4, C)
        ST = both(CH0 + 7168, 4, C)
        YD = [view(M0 + 2048, 4, 2 * T), view(H0, 4, 2 * T)]
        PE_A, PE_T, PE_G, PE_V, PE_L, PE_X, PE_U, PE_Y, PE_D = 1, 2, 3, 4, 4, 15, 16, 17, 18
        ACT_A, ACT_T, ACT_V, ACT_L, ACT_X, ACT_Y = 1, 2, 3, 3, 9, 10
        DVE_T, DVE_G, DVE_L, DVE_U, DVE_S = 1, 2, 2, 8, 9
        POOL_C, POOL_R, POOL_L = 1, 2, 2
        NM = {"pe": 18, "act": 10, "dve": 9, "pool": 7}

        def recurrence(E):
            base = E.wk

            def at(who, n, m, back=0):
                w = NM[who]
                return n * w + (w * (base + 1 - back) + m)

            if E.wk == 0:
                for d in range(2):
                    E.e.drain().then_inc(wk[E.name][d], NM[E.name])
            if E.name == "pool":
                for d in range(2):
                    E.e.memset(ST[d], 0.0)
            phase(E)

            tiles = [(p, h) for p in range(4) for h in range(2)]

            def rows(h):
                return slice(h * C, (h + 1) * C)

            def quad(b, at=0):
                return b[:, at:at + 4 * C].rearrange("p (a c) -> p a c", a=4)

            def chunk(n, o):
                if E.name == "pool":
                    for d in range(2):
                        E.e.wait_ge(wk["pe"][d], at("pe", n, PE_V, 1))
                        gs = slice(4 * d, 4 * d + 4)
                        oo = cols(o[d], C)
                        E.e.tensor_copy(LB[d][0:C], KB[0:C, gs, :, oo])
                        E.e.drain()
                        E.e.tensor_copy(LB[d][C:P, :, 0, :], KB[C:P, gs, 1, oo])
                        E.e.tensor_copy(LB[d][C:P, :, 1, :], KB[C:P, gs, 0, oo])
                        E.e.drain()
                        E.e.tensor_copy(VC[d], US[:, 8:12, oo])
                    for x, used in ((0, PE_X), (1, PE_Y)):
                        for d in range(2):
                            E.e.wait_ge(wk["pe"][d], at("pe", n, used, 1))
                            gs = slice(4 * d, 4 * d + 4)
                            E.e.tensor_copy(QC[d][:, :, x, :], QK[:, gs, x, cols(o[d], C)]).then_inc(wk["pool"][d], 1)
                    for lv in range(1, LEVELS):
                        for d in range(2):
                            E.e.wait_ge(wk["act"][d], at("act", n, ACT_A))
                            if lv >= 3:
                                E.e.wait_ge(wk["pe"][d], at("pe", n, PE_L + 2 * (lv - 2) - 1))
                            E.e.tensor_tensor(AM[d][:, lv % 2], AN[d][:, 0],
                                                      inv[:, d, lv:lv + 1, :].broadcast_to([P, 4, C]), ALU.mult).then_inc(wk["pool"][d], 1)
                if E.name == "pe":
                    for d in range(2):
                        B = bank[4 * d:4 * d + 4]
                        E.e.wait_ge(wk["pool"][d], at("pool", n, POOL_C))
                        E.e.wait_ge(wk["act"][d], at("act", n, ACT_X, 1))
                        settled(E)
                        for p, h in tiles:
                            r = rows(h)
                            b = LB[d][r, p, 1 - h, :]
                            E.e.matmul(B[2][r, p * C:(p + 1) * C], b, QC[d][r, p, 0, :], start=True, stop=True)
                            mm = E.e.matmul(B[2][r, (4 + p) * C:(5 + p) * C], QC[d][r, p, 0, :], b, start=True, stop=True)
                        mm.then_inc(wk["pe"][d], 1)
                        E.e.wait_ge(wk["dve"][d], at("dve", n, DVE_U, 1))
                        settled(E)
                        for p in range(4):
                            mm = E.e.transpose(B[3][:, p * P:(p + 1) * P], LB[d][:, p].rearrange("p a c -> p (a c)"), ident)
                        mm.then_inc(wk["pe"][d], 1)
                        E.e.wait_ge(wk["act"][d], at("act", n, ACT_Y, 1))
                        E.e.wait_ge(wk["dve"][d], at("dve", n, DVE_S, 1))
                        E.e.wait_ge(wk["pool"][d], at("pool", n, POOL_R))
                        settled(E)
                        for p, h in tiles:
                            r = rows(h)
                            mm = E.e.matmul(B[h][:, p * P:(p + 1) * P], LB[d][r, p].rearrange("p a c -> p (a c)"),
                                            QC[d][r, p].rearrange("p a c -> p (a c)"), start=True, stop=True)
                        mm.then_inc(wk["pe"][d], 1)
                    for d in range(2):
                        B = bank[4 * d:4 * d + 4]
                        E.e.wait_ge(wk["act"][d], at("act", n, ACT_T))
                        settled(E)
                        for p, h in tiles:
                            r = rows(h)
                            mm = E.e.matmul(B[3][r, p * C:(p + 1) * C], VC[d][r, p, :], eye64[r, :], start=True, stop=True)
                        mm.then_inc(wk["pe"][d], 1)
                    for lv in range(1, LEVELS):
                        for d in range(2):
                            B = bank[4 * d:4 * d + 4]
                            E.e.wait_ge(wk["pool"][d], at("pool", n, POOL_L + lv))
                            E.e.wait_ge(wk["dve"][d], at("dve", n, DVE_T if lv == 1 else DVE_L + lv - 1))
                            E.e.wait_ge(wk["act"][d], at("act", n, ACT_A if lv == 1 else ACT_L + lv - 1))
                            settled(E)
                            for p, h in tiles:
                                r = rows(h)
                                mm = E.e.matmul(B[2][r, p * C:(p + 1) * C], AM[d][r, lv % 2, p, :], TN[d][r, 1, p, :],
                                                start=True, stop=True)
                            mm.then_inc(wk["pe"][d], 1)
                        for d in range(2):
                            B = bank[4 * d:4 * d + 4]
                            E.e.wait_ge(wk["act"][d], at("act", n, ACT_L + lv))
                            E.e.wait_ge(wk["dve"][d], at("dve", n, DVE_G))
                            settled(E)
                            for p, h in tiles:
                                r = rows(h)
                                mm = E.e.matmul(B[0][r, p * C:(p + 1) * C], P1[d][r, p, :], TN[d][r, 0, p, :],
                                                start=True, stop=True)
                                if lv < LEVELS - 1:
                                    mm = E.e.matmul(B[0][r, (4 + p) * C:(5 + p) * C], TN[d][r, 0, p, :], P1[d][r, p, :],
                                                    start=True, stop=True)
                            mm.then_inc(wk["pe"][d], 1)
                    for d in range(2):
                        B = bank[4 * d:4 * d + 4]
                        E.e.wait_ge(wk["act"][d], at("act", n, ACT_L + LEVELS - 1))
                        E.e.wait_ge(wk["dve"][d], at("dve", n, DVE_S, 1))
                        settled(E)
                        for p, h in tiles:
                            r = rows(h)
                            E.e.matmul(B[2][r, p * C:(p + 1) * C], Gm[d][r, h, p, 0:C], UV[d][r, p, h, :], start=True, stop=False)
                            mm = E.e.matmul(B[2][r, p * C:(p + 1) * C], QC[d][r, p, 0, :], ST[d][r, p, :], start=False, stop=True)
                        mm.then_inc(wk["pe"][d], 1)
                    for d in range(2):
                        B = bank[4 * d:4 * d + 4]
                        E.e.wait_ge(wk["act"][d], at("act", n, ACT_X))
                        E.e.wait_ge(wk["dve"][d], at("dve", n, DVE_L + LEVELS - 1))
                        settled(E)
                        for p, h in tiles:
                            mm = E.e.matmul(B[3][rows(1 - h), p * C:(p + 1) * C], TN[d][rows(h), 0, p, :], XN[d][rows(h), p, :],
                                            start=True, stop=True)
                        mm.then_inc(wk["pe"][d], 1)
                    for d in range(2):
                        B = bank[4 * d:4 * d + 4]
                        E.e.wait_ge(wk["dve"][d], at("dve", n, DVE_U))
                        settled(E)
                        for p, h in tiles:
                            E.e.matmul(B[0][rows(h), p * C:(p + 1) * C], UV[d][:, p, h, :], Gm[d][:, h, p, C:P],
                                       start=(p == 0), stop=False, skip_group_check=True)
                        for p, h in tiles:
                            r = rows(h)
                            mm = E.e.matmul(B[0][r, p * C:(p + 1) * C], ST[d][r, p, :], QC[d][r, p, 1, :],
                                            start=False, stop=True, skip_group_check=True)
                        mm.then_inc(wk["pe"][d], 1)
                        for p, h in tiles:
                            mm = E.e.matmul(B[1][rows(h), p * C:(p + 1) * C], LT[d][:, p, rows(h)], UV[d][:, p, h, :],
                                            start=True, stop=True)
                        mm.then_inc(wk["pe"][d], 1)
                if E.name == "act":
                    for d in range(2):
                        B = bank[4 * d:4 * d + 4]
                        E.e.wait_ge(wk["pe"][d], at("pe", n, PE_A))
                        E.e.wait_ge(wk["pool"][d], at("pool", n, POOL_L + LEVELS - 1, 1))
                        E.e.wait_ge(wk["dve"][d], at("dve", n, DVE_T, 1))
                        E.e.activation(AN[d], B[2][:, :].rearrange("p (x a c) -> p x a c", x=2, a=4), ACT.Copy).then_inc(wk["act"][d], 1)
                        E.e.wait_ge(wk["pe"][d], at("pe", n, PE_T))
                        E.e.activation(LT[d], B[3][:, :].rearrange("p (a c) -> p a c", a=4), ACT.Copy).then_inc(wk["act"][d], 1)
                    for d in range(2):
                        B = bank[4 * d:4 * d + 4]
                        E.e.wait_ge(wk["pe"][d], at("pe", n, PE_V))
                        E.e.activation(UV[d][0:C, :, 0, :], quad(B[3])[0:C], ACT.Copy)
                        E.e.activation(UV[d][C:P, :, 1, :], quad(B[3])[C:P], ACT.Copy).then_inc(wk["act"][d], 1)
                    for lv in range(1, LEVELS):
                        for d in range(2):
                            E.e.wait_ge(wk["pe"][d], at("pe", n, PE_L + 2 * lv - 1))
                            E.e.activation(P1[d], quad(bank[4 * d + 2]), ACT.Copy, scale=-1.0).then_inc(wk["act"][d], 1)
                    for d in range(2):
                        E.e.wait_ge(wk["pe"][d], at("pe", n, PE_X))
                        E.e.activation(XN[d], quad(bank[4 * d + 2]), ACT.Copy, scale=-1.0).then_inc(wk["act"][d], 1)
                    for d in range(2):
                        E.e.wait_ge(wk["pe"][d], at("pe", n, PE_Y))
                        E.e.activation(YD[d][:, :, cols(o[d], C)], quad(bank[4 * d]), ACT.Copy).then_inc(wk["act"][d], 1)
                if E.name == "dve":
                    for d in range(2):
                        B = bank[4 * d:4 * d + 4]
                        E.e.wait_ge(wk["act"][d], at("act", n, ACT_A))
                        E.e.wait_ge(wk["pe"][d], at("pe", n, PE_U, 1))
                        E.e.tensor_tensor(TN[d], AN[d], neg0[:, d].unsqueeze(2).broadcast_to([P, 2, 4, C]), ALU.mult)
                        E.e.drain()
                        flat = TN[d].rearrange("p x a c -> p (x a) c")
                        E.e.tensor_tensor(flat, flat, eye64.unsqueeze(1).broadcast_to([P, 8, C]), ALU.add).then_inc(wk["dve"][d], 1)
                        E.e.wait_ge(wk["pe"][d], at("pe", n, PE_G))
                        for h in range(2):
                            ins = E.e.tensor_tensor(Gm[d][:, h], B[h][:, :].rearrange("p (a c) -> p a c", a=4),
                                                    m1[:, d:d + 1, :].broadcast_to([P, 4, P]), ALU.mult)
                        ins.then_inc(wk["dve"][d], 1)
                    for lv in range(1, LEVELS):
                        x = 2 if lv < LEVELS - 1 else 1
                        for d in range(2):
                            E.e.wait_ge(wk["pe"][d], at("pe", n, PE_L + 2 * lv))
                            t = TN[d][:, 0:x].rearrange("p x a c -> p (x a c)")
                            E.e.tensor_tensor(t, bank[4 * d][:, 0:x * 4 * C], t, ALU.add).then_inc(wk["dve"][d], 1)
                    for d in range(2):
                        B = bank[4 * d:4 * d + 4]
                        E.e.wait_ge(wk["pe"][d], at("pe", n, PE_U))
                        E.e.tensor_copy(UV[d][C:P, :, 0, :], quad(B[3])[C:P])
                        E.e.tensor_copy(UV[d][0:C, :, 1, :], quad(B[3])[0:C]).then_inc(wk["dve"][d], 1)
                    for d in range(2):
                        E.e.wait_ge(wk["pe"][d], at("pe", n, PE_D))
                        E.e.tensor_tensor(ST[d], ST[d], quad(bank[4 * d + 1]), ALU.add)
                        E.e.drain()
                        turn = n if d == 0 else n * -1 + 7
                        E.e.tensor_tensor(ST[d], ST[d], FS[:, d, :, one(turn)].broadcast_to([P, 4, C]), ALU.mult).then_inc(wk["dve"][d], 1)

            with E.e.Fori(0, 2) as seg:
                with E.e.Fori(0, 4) as j:
                    chunk(seg * 4 + j, (seg * -T + j * C + T, seg * -T + j * -C + (2 * T - C)))
            E.wk += NCH
            phase(E)

        def mix_out(E, l):
            N = 2 * T if l == 0 else T
            if E.name == "dve":
                for k in range(4):
                    E.e.tensor_tensor(MIXF[:, 4 + k, 0:N], MIXF[:, 4 + k, 0:N], view(H0, 4, 2 * T)[:, k, 0:N], ALU.add)
            phase(E)

            def order(ap):
                return ap if l == 0 else column_major(ap)

            def natural(ap):
                return ap if l == 0 else by_four(ap)

            cen = view(R0, 4, N)
            head_norm(E, lambda k: MIXF[:, k, 0:N], N, LN_EPS, R0)
            if E.name == "act":
                for k in range(4):
                    E.e.activation(order(MIXF[:, k, 0:N]), natural(cen[:, k, :]), ACT.Silu,
                                   scale=par(l, "cng", 4)[:, k:k + 1], bias=par(l, "cnb", 4)[:, k:k + 1])
            head_norm(E, lambda k: MIXF[:, 4 + k, 0:N], N, GN_EPS, R0 + 4096)
            cen2 = view(R0 + 4096, 4, N)
            if E.name == "dve":
                for k in range(4):
                    E.e.tensor_scalar(cen2[:, k, :], cen2[:, k, :], par(l, "gng", 4)[:, k:k + 1],
                                      par(l, "gnb", 4)[:, k:k + 1], ALU.mult, ALU.add)
                E.e.drain()
                for k in range(4):
                    E.e.tensor_tensor(cen2[:, k, :], cen2[:, k, :], US[:, k, 0:N], ALU.add)
                E.e.drain()
                for k in range(4):
                    E.e.tensor_tensor(order(MIXF[:, 4 + k, 0:N]), natural(cen2[:, k, :]), natural(US[:, 4 + k, 0:N]), ALU.mult)
            phase(E)

        def gated_residual(E, l, m, N):
            def fn(u, b):
                for s in range(N // T):
                    x = XF[:, one(u), s * T:(s + 1) * T].rearrange("p o t -> p (o t)")
                    ins = E.e.scalar_tensor_tensor(out=x, in0=b[:, s * T:(s + 1) * T], scalar=MOD[l][:, one(m + u), s],
                                                   in1=x, op0=ALU.mult, op1=ALU.add)
                return ins
            return fn

        def up_down(E, N, rhs, residual):
            hid = view(R0, KF, N)
            tmp = view(CH0, 2, 512)
            if E.name == "pe":
                gemm_pe(E, 2 * KF, KD, 8, rhs, N, "free_dve")
            if E.name == "act":
                gated_act(E, 2 * KF, ACT.Silu, N, tmp)
            if E.name == "dve":
                gated_dve(E, 2 * KF, lambda p: hid[:, one(p), :].rearrange("p o t -> p (o t)"), N, tmp)
            units_done(E, 2 * KF, "free_dve", KF)
            phase(E)
            if E.name == "pe":
                gemm_pe(E, KD, KF, 11, lambda k: hid[:, k, :], N, "free_dve")
            if E.name == "dve":
                take_units(E, "free_dve", KD, residual)
            units_done(E, KD, "free_dve")
            phase(E)

        def first_layer_stages(E, l):
            N = 2 * T if l == 0 else T
            rms(E, 2 * T, lambda k, s: GS[2 * l][:, k, s:s + 1], lambda k, s: MOD[l][:, k, s:s + 1], HF)
            input_projection(E, l)
            rwkv_prep(E, l)
            recurrence(E)
            mix_out(E, l)
            if E.name == "pe":
                gemm_pe(E, KD, KD, 8, lambda k: MIXF[:, k, 0:N], N, "free_dve")
            if E.name == "dve":
                take_units(E, "free_dve", KD, gated_residual(E, l, 16, N))
            units_done(E, KD, "free_dve")
            phase(E)
            rms(E, N, lambda k, s: GS[2 * l + 1][:, k, s:s + 1], lambda k, s: MOD[l][:, 24 + k, s:s + 1], HF)
            up_down(E, N, lambda k: HF[:, k, 0:N], gated_residual(E, l, 40, N))

        XT = XF[:, :, 0:T]
        CUR = view(MOD0, QN + 8)
        LBND = view(MOD0 + 80, 2, 2, 4)
        lb_e = view(MOD0 + 96, 2, 4)
        lb_m = view(MOD0 + 104, 4)
        FB = view(MOD0 + 112, 4 * NB)
        F, K_, Q, I = (view(U0 + n * 1024, HH, T) for n in range(4))
        ZG, ZU, ZV = (view(U0 + n * 1024, HH, T) for n in range(4, 7))
        SZ = view(M0, 16, T)
        YB = view(R0, 64 * HB * (HB + 1) // 2)
        KE = [view(R0 + 8704 + n * 1024, 64, HB) for n in range(2)]
        PR, SU = (view(R0 + 10752 + n * 1024, 64, HB) for n in range(2))
        KH = [view(R0 + 12800 + n * 1024, HH, T) for n in range(2)]
        PS = view(CH0, HH, 2 * T)
        VT = view(CH0 + 2048, 2, 512)
        IT = view(H0, 2, 512)
        O = view(H0 + 1024, HH, T)
        ZT = view(H0 + 2048, 2, 512)
        WS = view(H0 + 3072, 4, P)
        BS = view(H0 + 3584, 4, P)
        LN_SCR = CH0 + 3072

        def blocks(v):
            return v.rearrange("p h (b j) -> p (h b) j", j=HB)

        def lower_bounds(E):
            if E.name == "dve":
                E.e.tensor_tensor(lb_m, hg_lb[:, 0, :], hg_lb[:, 1, :], ALU.max)
                E.e.drain()
                for l in range(2):
                    E.e.tensor_tensor(lb_e[:, l, :], hg_lb[:, l, :], lb_m, ALU.subtract)
                E.e.drain().then_inc(S["dve_step"], 1)
                E.e.wait_ge(S["act_step"], E.v("act_step", 1))
                E.e.tensor_tensor(lb_m, lb_e[:, 0, :], lb_e[:, 1, :], ALU.add)
                E.e.drain()
                E.e.reciprocal(lb_m, lb_m)
                E.e.drain()
                for l in range(2):
                    E.e.tensor_tensor(lb_e[:, l, :], lb_e[:, l, :], lb_m, ALU.mult)
                E.e.drain()
                E.e.tensor_tensor(LBND[:, 1, 0, :], lb_e[:, 0, :], lb_e[:, 1, :], ALU.add)
                E.e.tensor_tensor(LBND[:, 0, 0, :], lb_e[:, 0, :], lb_e[:, 0, :], ALU.subtract)
                E.e.drain()
                E.e.tensor_tensor(LBND[:, 1, 0, :], LBND[:, 1, 0, :], lb_e[:, 0, :], ALU.subtract)
                E.e.drain()
                E.e.tensor_scalar(LBND[:, :, 1, :], LBND[:, :, 0, :], -1.0, 1.0, ALU.mult, ALU.add)
            if E.name == "act":
                E.e.wait_ge(S["dve_step"], E.v("dve_step", 1))
                E.e.activation(lb_e, lb_e, ACT.Exp).then_inc(S["act_step"], 1)
            steps(E, act=1, dve=1)
            phase(E)

        def cur(name, n):
            return CUR[:, QCOL[name] + n:QCOL[name] + n + 1]

        def bound(h):
            return CUR[:, QN + h:QN + h + 1]

        def layer_start(E, l):
            if E.name == "dve":
                E.e.tensor_copy(CUR[:, 0:QN].unsqueeze(1), arena[:, P2:P2 + 2 * QN].rearrange("p (l n) -> p l n", l=2)[:, one(l), :])
                E.e.tensor_copy(CUR[:, QN:QN + 8].unsqueeze(1), LBND.rearrange("p l a b -> p l (a b)")[:, one(l), :])
            if E.name == "act":
                E.e.dma_start(WS, a["sg_ws"][one(l)].rearrange("o p g t -> p (o g) t")).then_inc(S["layer_in"], 16)
                E.e.dma_start(BS[0:1], a["sg_bs"][one(l)]).then_inc(S["layer_in"], 16)
            E.c["layer_in"] += 32
            phase(E)

        def scaled_residual(E, scale):
            def fn(u, b):
                x = XT[:, one(u), :].rearrange("p o t -> p (o t)")
                return E.e.scalar_tensor_tensor(out=x, in0=b[:, 0:T], scalar=scale, in1=x, op0=ALU.mult, op1=ALU.add)
            return fn

        def macaron(E, n):
            hid = view(R0, KF, T)
            tmp = view(CH0, 2, 512)
            if E.name == "pe":
                gemm_pe(E, 2 * KF, KD, 8, lambda k: XT[:, k, :], T, "free_dve")
            if E.name == "act":
                gated_act(E, 2 * KF, ACT.Silu, T, tmp)
            if E.name == "dve":
                gated_dve(E, 2 * KF, lambda p: hid[:, one(p), :].rearrange("p o t -> p (o t)"), T, tmp)
            units_done(E, 2 * KF, "free_dve", KF)
            phase(E)
            if E.name == "pe":
                gemm_pe(E, KD, KF, 11, lambda k: hid[:, k, :], T, "free_dve")
            if E.name == "dve":
                for k in range(KD):
                    E.e.tensor_scalar(XT[:, k, :], XT[:, k, :], ALPHA, None, ALU.mult)
                E.e.drain()
                take_units(E, "free_dve", KD, scaled_residual(E, 0.5))
            units_done(E, KD, "free_dve")
            phase(E)
            layer_norm(E, lambda k: XT[:, k, :], lambda k: XT[:, k, :], KD,
                       lambda k: cur("lng", 8 * n + k), lambda k: cur("lnb", 8 * n + k), LN_SCR)

        def mixer_input(E):
            if E.name == "pe":
                gemm_pe(E, 40, KD, 8, lambda k: XT[:, k, :], T, "free_act")
            if E.name == "act":
                def group(first, n, fn):
                    E.c["bank_full"] += first
                    E.c["free_act"] += first
                    take_units(E, "free_act", n, fn)
                    E.c["bank_full"] -= first
                    E.c["free_act"] -= first

                def forget(u, b):
                    E.e.activation(F[:, u, :], b[:, 0:T], ACT.Sigmoid)
                    return E.e.activation(K_[:, u, :], b[:, 0:T], ACT.Sigmoid, scale=-1.0)

                def into(dst, func):
                    return lambda u, b: E.e.activation(dst[:, one(u), :].rearrange("p o t -> p (o t)"), b[:, 0:T], func)
                group(0, 4, forget)
                group(4, 4, into(I, ACT.Copy))
                group(8, 4, into(Q, ACT.Copy))
                E.e.drain().then_inc(S["act_step"], 1)
                group(12, 4, into(ZG, ACT.Silu))
                group(16, 4, into(ZU, ACT.Gelu_apprx_tanh))
                group(20, 4, into(ZV, ACT.Gelu_apprx_tanh))
                group(24, 16, into(SZ, ACT.Sigmoid))
            units_done(E, 40, "free_act")
            if E.name == "pool":
                for n in range(2):
                    E.e.memset(KH[n], 0.0)
                E.e.wait_ge(S["layer_in"], E.v("layer_in", 0))
                for g in range(4):
                    E.e.tensor_tensor(WS[:, g, :], WS[:, g, :], tril, ALU.mult)
            if E.name == "dve":
                E.e.wait_ge(S["act_step"], E.v("act_step", 1))
                for h in range(HH):
                    E.e.tensor_scalar(F[:, h, :], F[:, h, :], bound(4 + h), bound(h), ALU.mult, ALU.add)
                    E.e.tensor_scalar(K_[:, h, :], K_[:, h, :], bound(4 + h), None, ALU.mult)
                E.e.drain()
                f, k, q = blocks(F), blocks(K_), blocks(Q)
                E.e.tensor_copy(PR[:, :, 0:1], f[:, :, 0:1])
                E.e.memset(SU[:, :, HB - 1:HB], 1.0)
                for j in range(1, HB):
                    E.e.drain()
                    E.e.tensor_tensor(PR[:, :, j:j + 1], PR[:, :, j - 1:j], f[:, :, j:j + 1], ALU.mult)
                    E.e.tensor_tensor(SU[:, :, HB - 1 - j:HB - j], SU[:, :, HB - j:HB - j + 1], f[:, :, HB - j:HB - j + 1], ALU.mult)
                E.e.drain()
                E.e.tensor_copy(FB.unsqueeze(2), PR[:, :, HB - 1:HB])
                E.e.drain()
                E.e.tensor_tensor(PR, PR, q, ALU.mult)
                E.e.tensor_tensor(SU, SU, k, ALU.mult)
                at = 0
                for lag in range(HB):
                    n = HB - lag
                    ke = KE[lag % 2]
                    if lag == 0:
                        E.e.tensor_copy(ke, k)
                    else:
                        E.e.tensor_tensor(ke[:, :, lag:HB], KE[1 - lag % 2][:, :, lag - 1:HB - 1], f[:, :, lag:HB], ALU.mult)
                    E.e.drain()
                    y = YB[:, at:at + 64 * n].rearrange("p (b j) -> p b j", j=n)
                    E.e.tensor_tensor(y, ke[:, :, lag:HB], q[:, :, lag:HB], ALU.mult)
                    at += 64 * n
            steps(E, act=1)
            phase(E)

        def spatial_gate(E):
            layer_norm(E, lambda k: ZV[:, k, :], lambda k: ZV[:, k, :], 4,
                       lambda k: cur("slg", k), lambda k: cur("slb", k), LN_SCR)
            if E.name == "pe":
                for x, src in ((0, ZV), (1, I)):
                    for n in range(2):
                        for g in range(4):
                            mm = E.e.transpose(bank[2 * x + n][:, g * P:(g + 1) * P], src[:, g, n * P:(n + 1) * P], ident)
                        mm.then_inc(S["pe_step"], 1)
                E.e.wait_ge(S["layer_in"], E.v("layer_in", 0))
                E.e.wait_ge(S["act_step"], E.v("act_step", 2))
                for g in range(4):
                    for n in range(2):
                        o = bank[4 + g // 2][:, (g % 2) * T + n * P:(g % 2) * T + (n + 1) * P]
                        E.e.matmul(o, VT[:, n, g * P:(g + 1) * P], WS[:, g, :], start=True, stop=False)
                        mm = E.e.matmul(o, ones[0:1, :], BS[0:1, g, :], start=False, stop=True)
                mm.then_inc(S["pe_step"], 1)
            if E.name == "act":
                for n in range(4):
                    E.e.wait_ge(S["pe_step"], E.v("pe_step", n + 1))
                    E.e.activation((VT if n < 2 else IT)[:, n % 2, :], bank[n][:, :], ACT.Copy).then_inc(S["act_step"], 1)
            if E.name == "dve":
                E.e.wait_ge(S["pe_step"], E.v("pe_step", 5))
                for x in range(2):
                    u = ZU[:, 2 * x:2 * x + 2, :].rearrange("p h t -> p (h t)")
                    E.e.tensor_tensor(u, u, bank[4 + x][:, :], ALU.mult)
            steps(E, pe=5, act=4)
            phase(E)

        def hgrn(E):
            if E.name == "dve":
                def block_step(n, buf):
                    E.e.wait_ge(S["pe_step"], E.v("pe_step", n - 1))
                    for h in range(HH):
                        E.e.tensor_scalar(KH[buf][:, h, :], KH[1 - buf][:, h, :], FB[:, one(n - 1 + h * NB)], None, ALU.mult)
                    E.e.drain()
                    for h in range(HH):
                        ins = E.e.tensor_copy(KH[buf][:, h, cols((n - 1) * HB, HB)],
                                              SU[:, one(n - 1 + h * NB), :].rearrange("p o j -> p (o j)"))
                    ins.then_inc(S["dve_step"], 1)
                    E.e.drain()
                with E.e.Fori(0, 7) as i:
                    block_step(i * 2 + 1, 1)
                    block_step(i * 2 + 2, 0)
                block_step(15, 1)
            if E.name == "pe":
                def block_use(n, buf):
                    E.e.wait_ge(S["dve_step"], E.v("dve_step", n))
                    for h in range(HH):
                        for x in range(2):
                            mm = E.e.matmul(bank[4 + h][:, cols(n * HB + x * T, HB)], KH[buf][:, h, x * P:(x + 1) * P],
                                            PR[:, one(n + h * NB), :].rearrange("p o j -> p (o j)"), start=True, stop=True)
                    mm.then_inc(S["pe_step"], 1)
                block_use(0, 0)
                with E.e.Fori(0, 7) as i:
                    block_use(i * 2 + 1, 1)
                    block_use(i * 2 + 2, 0)
                block_use(15, 1)
            if E.name == "act":
                E.e.wait_ge(S["pe_step"], E.v("pe_step", 16))
                for h in range(HH):
                    E.e.activation(PS[:, h, :], bank[4 + h][:, :], ACT.Copy).then_inc(S["act_step"], 1)
            steps(E, pe=16, act=4, dve=15)
            if E.name == "pe":
                E.e.wait_ge(S["act_step"], E.v("act_step", 0))
                for h in range(HH):
                    for x in range(2):
                        mm = E.e.matmul(bank[h // 2][:, (h % 2) * T:(h % 2 + 1) * T], IT[:, x, h * P:(h + 1) * P],
                                        PS[:, h, x * T:(x + 1) * T], start=(x == 0), stop=(x == 1))
                mm.then_inc(S["pe_step"], 1)
                at, u = 0, 0
                for lag in range(HB):
                    n = 32 * (HB - lag)
                    for x in range(2):
                        if u >= 6:
                            E.e.wait_ge(S["dve_step"], E.v("dve_step", u - 5))
                        E.e.matmul(bank[2 + u % 6][:, 0:n], ones, YB[:, at:at + n], start=True, stop=True).then_inc(S["pe_step"], 1)
                        at += n
                        u += 1
            if E.name == "dve":
                i = blocks(I)
                o = blocks(O)
                u = 0
                for lag in range(HB):
                    n = HB - lag
                    for x in range(2):
                        E.e.wait_ge(S["pe_step"], E.v("pe_step", 2 + u))
                        b = bank[2 + u % 6][:, 0:32 * n].rearrange("p (b j) -> p b j", j=n)
                        bs = slice(32 * x, 32 * x + 32)
                        z = (o if lag == 0 else ZT[:, x, :].rearrange("p (b j) -> p b j", j=HB))
                        z = z[:, bs, :] if lag == 0 else z[:, :, 0:n]
                        E.e.tensor_tensor(z, b, i[:, bs, 0:n], ALU.mult).then_inc(S["dve_step"], 1)
                        u += 1
                    E.e.drain()
                    if lag:
                        for x in range(2):
                            bs = slice(32 * x, 32 * x + 32)
                            z = ZT[:, x, :].rearrange("p (b j) -> p b j", j=HB)[:, :, 0:n]
                            E.e.tensor_tensor(o[:, bs, lag:HB], o[:, bs, lag:HB], z, ALU.add)
                        E.e.drain()
                for x in range(2):
                    oo = O[:, 2 * x:2 * x + 2, :].rearrange("p h t -> p (h t)")
                    E.e.tensor_tensor(oo, oo, bank[x][:, :], ALU.add)
            steps(E, pe=33, dve=32)
            phase(E)
            if E.name == "act":
                for x in range(2):
                    E.e.activation(ZT[:, x, :], O[:, 2 * x:2 * x + 2, :].rearrange("p h t -> p (h t)"), ACT.Square).then_inc(S["act_step"], 1)
                for x in range(2):
                    E.e.wait_ge(S["dve_step"], E.v("dve_step", x + 1))
                    E.e.activation(ZT[:, x, :], ZT[:, x, :], ACT.Sqrt).then_inc(S["act_step"], 1)
            if E.name == "pe":
                for x in range(2):
                    E.e.wait_ge(S["act_step"], E.v("act_step", x + 1))
                    E.e.matmul(bank[x][:, :], ones, ZT[:, x, :], start=True, stop=True).then_inc(S["pe_step"], 1)
            if E.name == "dve":
                E.e.wait_ge(S["pe_step"], E.v("pe_step", 2))
                rstd_dve(E, [(bank[x][:, :], ZT[:, x, :]) for x in range(2)], 1.0 / P, RMS_EPS)
                E.e.wait_ge(S["act_step"], E.v("act_step", 4))
                for h in range(HH):
                    E.e.scalar_tensor_tensor(out=O[:, h, :], in0=O[:, h, :], scalar=cur("ng", h),
                                             in1=ZT[:, h // 2, (h % 2) * T:(h % 2 + 1) * T], op0=ALU.mult, op1=ALU.mult)
                E.e.drain()
                E.e.tensor_tensor(O.rearrange("p h t -> p (h t)"), O.rearrange("p h t -> p (h t)"),
                                  ZG.rearrange("p h t -> p (h t)"), ALU.mult)
            steps(E, pe=2, act=4, dve=2)
            phase(E)

        def mixer_output(E):
            for x, src in ((0, O), (1, ZU)):
                if E.name == "pe":
                    gemm_pe(E, KD, 4, 8, lambda k: src[:, k, :], T, "free_dve", body=8)
                if E.name == "dve":
                    def fn(u, b):
                        return E.e.tensor_tensor(SZ[:, 8 * x + u, :], SZ[:, 8 * x + u, :], b[:, 0:T], ALU.mult)
                    take_units(E, "free_dve", KD, fn, body=8)
                units_done(E, KD, "free_dve")
            if E.name == "dve":
                E.e.drain()
                for k in range(KD):
                    E.e.tensor_tensor(SZ[:, k, :], SZ[:, k, :], SZ[:, 8 + k, :], ALU.add)
                    E.e.tensor_scalar(XT[:, k, :], XT[:, k, :], ALPHA, None, ALU.mult)
            phase(E)
            if E.name == "pe":
                gemm_pe(E, KD, KD, 8, lambda k: SZ[:, k, :], T, "free_dve")
            if E.name == "dve":
                take_units(E, "free_dve", KD, scaled_residual(E, 1.0))
            units_done(E, KD, "free_dve")
            phase(E)
            layer_norm(E, lambda k: XT[:, k, :], lambda k: XT[:, k, :], KD,
                       lambda k: cur("lng", 8 + k), lambda k: cur("lnb", 8 + k), LN_SCR)

        def program(E):
            if E.name == "pe":
                E.e.drain().then_inc(S["slab_used"], RING - 1)
            if E.name == "dve":
                E.e.drain().then_inc(S["free_dve"], 4)
            if E.name == "act":
                E.e.drain().then_inc(S["free_act"], 4)
            E.e.wait_ge(S["consts_in"], 16 * 4)
            modulation_start(E)
            for l in range(DEPTH):
                first_layer_stages(E, l)
            rms(E, T, lambda k, s: final_g[:, k:k + 1], None, XF)
            lower_bounds(E)
            before = dict(E.c)
            slab = E.slab
            with E.e.Fori(0, DEPTH) as l:
                E.l = l
                layer_start(E, l)
                macaron(E, 0)
                mixer_input(E)
                spatial_gate(E)
                hgrn(E)
                mixer_output(E)
                macaron(E, 2)
            E.l = None
            grown = {k: E.c[k] - before[k] for k in E.c}
            assert grown == PER, grown
            for k in E.c:
                E.c[k] = before[k] + DEPTH * PER[k]
            assert E.name != "pe" or E.slab - slab == SLABS2, E.slab - slab

        block = ctx.enter_context(nc.Block())

        @block.sync
        def _(sp):
            E = Eng(sp, "sp")
            sp.dma_start(cst, a["consts"]).then_inc(S["consts_in"], 16)
            sp.dma_start(arena[:, K0:K1], a["params"]).then_inc(S["consts_in"], 16)
            sp.dma_start(cond, a["cond"]).then_inc(S["consts_in"], 16)
            sp.dma_start(X, a["x"]).then_inc(S["consts_in"], 16)

            def rows_of(name, per):
                def src(at):
                    at = at if E.l is None else at + E.l * per
                    return a[name][one(at)].rearrange("o p w -> p (o w)")
                return src
            load_slabs(E, rows_of("ada_w", 0), ADA_FIRST, 8)
            for l in range(DEPTH):
                w_in, ada = rows_of("w_in", 0), rows_of("ada_w", 0)
                if l == 0:
                    def some(i, count):
                        for s in range(count):
                            slab_to_slot(E, s, i, 4, w_in(i) if s == 0 else ada(i * 3 + (ADA_FIRST + s - 1)), 8 * P)
                    repeat(E, 4 * 23, 4, some)
                    E.slab += 4 * 23
                else:
                    load_slabs(E, w_in, 23, 8, first=23)
                load_slabs(E, rows_of("w_out", 0), 8, 8, first=8 * l)
                load_slabs(E, rows_of("ffn_up", 0), 44, 8, first=44 * l)
                load_slabs(E, rows_of("ffn_down", 0), 16, 11, first=16 * l)
            with sp.Fori(0, DEPTH) as l:
                E.l = l
                load_slabs(E, rows_of("ffn1_up", 44), 44, 8)
                load_slabs(E, rows_of("ffn1_down", 16), 16, 11)
                load_slabs(E, rows_of("w_in_2", 40), 40, 8)
                load_slabs(E, rows_of("branches", 8), 8, 8)
                load_slabs(E, rows_of("w_out_2", 8), 8, 8)
                load_slabs(E, rows_of("ffn2_up", 44), 44, 8)
                load_slabs(E, rows_of("ffn2_down", 16), 16, 11)
            sp.wait_ge(S["store"], 1)
            sp.dma_start(out, XT).then_inc(S["x_in"], 16)
            sp.wait_ge(S["x_in"], 16)

        @block.tensor
        def _(pe):
            program(Eng(pe, "pe"))

        @block.scalar
        def _(act):
            program(Eng(act, "act"))
            act.drain().then_inc(S["store"], 1)

        @block.vector
        def _(dve):
            program(Eng(dve, "dve"))

        @block.gpsimd
        def _(pool):
            program(Eng(pool, "pool"))


PER = {"slab_used": 0, "bank_full": 168, "free_dve": 128, "free_act": 40, "act_ready": 44, "pe_phase": 15,
       "act_phase": 15, "dve_phase": 15, "pool_phase": 15, "pe_step": 64, "act_step": 45, "dve_step": 109,
       "pool_step": 0, "consts_in": 0, "layer_in": 32, "x_in": 0, "store": 0, "ada_full": 0, "ada_copied": 0}


def slabs(w, order, K, tiles):
    L, rows, N = w.shape
    n = len(order)
    pad = (max(order) + 1) * P - N
    if pad > 0:
        w = np.concatenate([w, np.zeros((L, rows, pad), w.dtype)], axis=2)
    t = w.reshape(L, K, P, w.shape[2] // P, P)[:, :, :, list(order), :]
    t = t.transpose(0, 3, 1, 2, 4).reshape(L * n * K // tiles, tiles, P, P)
    return np.ascontiguousarray(t.transpose(0, 2, 1, 3)).reshape(L * n * K // tiles, P, tiles * P)


def feature_columns(v, n):
    v = v.reshape(-1, v.shape[-1])
    pad = -v.shape[1] % P
    if pad:
        v = np.concatenate([v, np.zeros((v.shape[0], pad), v.dtype)], axis=1)
    return v.reshape(v.shape[0], -1, P)


def constants():
    s, t = np.arange(P)[:, None], np.arange(P)[None, :]
    out = {"ident": np.eye(P), "ones": np.ones((P, P)), "blk64": s // C == t // C}
    same = s // C == t // C
    sl, tl = s % C, t % C
    half = C // 2
    cum = np.zeros((P, 2, 2, P))
    cum[:, 0, 0] = same * ((sl <= tl) * 1.0 - (sl < half))
    cum[:, 0, 1] = same * ((sl < tl) * 1.0 - (sl < half))
    cum[:, 1, 0] = same * ((sl >= tl) * 1.0 - (sl >= half))
    cum[:, 1, 1] = same * ((sl > tl) * 1.0 - (sl >= half))
    out["cum"] = cum
    s1 = np.arange(P)[:, None] % C
    t1 = np.arange(C)[None, :]
    m1 = np.zeros((P, 2, P))
    m1[:, 0, :C], m1[:, 0, C:] = s1 < t1, s1 <= t1
    m1[:, 1, :C], m1[:, 1, C:] = s1 > t1, s1 >= t1
    out["m1"] = m1
    inv = np.zeros((P, 2, LEVELS, C))
    for lv in range(LEVELS):
        b = 1 << lv
        both = s1 // (2 * b) == t1 // (2 * b)
        inv[:, 0, lv] = both & (s1 // b % 2 == 0) & (t1 // b % 2 == 1)
        inv[:, 1, lv] = both & (s1 // b % 2 == 1) & (t1 // b % 2 == 0)
    out["inv"] = inv
    neg0 = np.zeros((P, 2, 2, C))
    for d in range(2):
        neg0[:, d, 0], neg0[:, d, 1] = -inv[:, d, 0], -inv[:, 1 - d, 0]
    out["neg0"] = neg0
    out["eye64"] = s1 == t1
    out["tril"] = s <= t
    out["pick"] = s % 32 == np.arange(2)[None, :]
    return np.concatenate([np.asarray(out[n], np.float32).reshape(P, -1) for n, _ in CONSTS], axis=1)


def kernel(**x):
    import concourse.bacc as bacc
    from concourse.bass_utils import run_bass_kernel_spmd

    x = {k: np.ascontiguousarray(v) for k, v in x.items()}
    ff = [j for p in range(KF) for j in (p, KF + p)]
    joined = np.concatenate([x["ffn_wg"], x["ffn_wu"]], axis=2)
    arrays = {
        "consts": constants(),
        "ada_w": slabs(x["ada_w"], range(48), KD, 8),
        "w_in": slabs(x["w_in"], [j for p in range(4) for j in (4 + p, p)] + list(range(8, 23)), KD, 8),
        "w_out": slabs(x["w_out"], range(8), KD, 8),
        "ffn_up": slabs(joined, ff, KD, 8),
        "ffn_down": slabs(x["ffn_wd"], range(8), KF, 11),
        "ffn1_up": slabs(x["ffn1_w13_2"], ff, KD, 8),
        "ffn1_down": slabs(x["ffn1_w2_2"], range(8), KF, 11),
        "ffn2_up": slabs(x["ffn2_w13_2"], ff, KD, 8),
        "ffn2_down": slabs(x["ffn2_w2_2"], range(8), KF, 11),
        "w_in_2": slabs(x["w_in_2"], [*range(4, 8), *range(8, 12), *range(0, 4), *range(12, 40)], KD, 8),
        "w_out_2": slabs(x["w_out_2"], range(8), KD, 8),
    }
    br = [slabs(x[n], range(8), 4, 8).reshape(DEPTH, 4, P, 8 * P) for n in ("w_branch_a_2", "w_branch_b_2")]
    arrays["branches"] = np.stack(br, axis=1).reshape(DEPTH * 8, P, 8 * P)
    xs = np.stack([x["x"][0], x["ctx"][0]])
    arrays["x"] = np.ascontiguousarray(xs.reshape(2, T, KD, P).transpose(3, 2, 0, 1))
    arrays["cond"] = np.ascontiguousarray(np.stack([x["c"][0], x["c_ctx"]]).reshape(2, KD, P).transpose(2, 1, 0))

    def chunked(v):
        return feature_columns(v, 0).transpose(2, 0, 1)

    cols_ = []
    for l in range(DEPTH):
        one = {"n1g": x["norm1_g"][l], "n2g": x["norm2_g"][l], "cb": x["conv_b"][l], "cng": x["cnorm_g"][l],
               "cnb": x["cnorm_b"][l], "ib0": x["iclr_b0"][l], "kk": x["k_k"][l], "ka": x["k_a"][l],
               "rk": x["r_k"][l], "gng": x["gn_g"][l], "gnb": x["gn_b"][l], "adab": x["ada_b"][l]}
        parts = {n: chunked(v).reshape(P, -1) for n, v in one.items()}
        parts["cw"] = chunked(x["conv_w"][l]).transpose(0, 2, 1).reshape(P, -1)
        parts["sw"] = chunked(x["shift_w"][l]).transpose(0, 2, 1).reshape(P, -1)
        cols_ += [parts[n] for n, k in PARAMS1 if k]
    cols_.append(chunked(x["final_g"]).reshape(P, -1))
    for l in range(DEPTH):
        parts = {"lng": x["ln_g_2"][l], "lnb": x["ln_b_2"][l], "ng": x["hg_norm_g_2"][l],
                 "slg": x["sg_ln_g_2"][l], "slb": x["sg_ln_b_2"][l]}
        cols_ += [chunked(parts[n]).reshape(P, -1) for n, _ in PARAMS2]
    cols_.append(chunked(x["hg_lb_2"]).reshape(P, -1))
    arrays["params"] = np.ascontiguousarray(np.concatenate(cols_, axis=1))
    arrays["decay_w"] = np.concatenate([x["decay_up"], x["decay_b0"][:, :, None, :]], axis=2).transpose(0, 2, 1, 3).reshape(DEPTH, 65, 1024)
    arrays["iclr_w"] = x["iclr_up"].transpose(0, 2, 1, 3).reshape(DEPTH, 64, 1024)
    g = np.concatenate([x["g_up"], np.zeros((DEPTH, 96, 512), np.float32)], axis=1)
    arrays["gate_w"] = g.reshape(DEPTH, 2, P, 512).transpose(0, 2, 1, 3)
    arrays["sg_ws"] = x["sg_ws_2"].transpose(0, 3, 1, 2)
    arrays["sg_bs"] = x["sg_bs_2"].reshape(DEPTH, 4, P)

    nc = bacc.Bacc("TRN2", target_bir_lowering=False, num_devices=1)
    ins = {}
    for n, v in arrays.items():
        arrays[n] = np.ascontiguousarray(v)
        ins[n] = nc.dram_tensor("in_" + n, v.shape, mybir.dt.from_np(v.dtype), kind="ExternalInput").ap()
    out = nc.dram_tensor("out_x", (P, KD, T), F32, kind="ExternalOutput").ap()
    build(nc, ins, out)
    r = run_bass_kernel_spmd(nc, [{"in_" + n: v for n, v in arrays.items()}], core_ids=[0])
    y = r.results[0]["out_x"]
    return np.ascontiguousarray(y.transpose(2, 1, 0)).reshape(1, T, D)
```

```python
from contextlib import ExitStack

import concourse.bass as bass
import numpy as np
from concourse import mybir
from concourse.alu_op_type import AluOpType as ALU

F32 = mybir.dt.float32
ACT = mybir.ActivationFunctionType

P = 128
D = 1024
KD = D // P
T = 256
FF = 2816
KF = FF // P
DEPTH = 2
CONV_K = 31
PAD = CONV_K // 2
ZW = T + 2 * PAD
RMS_EPS, LN_EPS, GN_EPS = 1e-6, 1e-5, 64e-5
KAPPA = 0.606531
ALPHA = (2 * DEPTH) ** 0.25
C = 64
NCH = 2 * T // C
LEVELS = 6
RING = 4
SLOT = 11 * P
SLABS2 = 2 * (2 * KF + 16) + 40 + 8 + 8
HB = 16
NB = T // HB
HH = 4

CONSTS = [("ident", P), ("ones", P), ("blk64", P), ("cum", 4 * P), ("m1", 2 * P), ("inv", 2 * LEVELS * C),
          ("neg0", 4 * C), ("eye64", C), ("tril", P), ("pick", 2)]
PARAMS1 = [("n1g", 8), ("n2g", 8), ("cw", 4 * CONV_K), ("cb", 4), ("cng", 4), ("cnb", 4), ("sw", 15 * 3),
           ("db0", 0), ("ib0", 8), ("kk", 4), ("ka", 4), ("rk", 4), ("gng", 4), ("gnb", 4), ("adab", 48)]
PARAMS2 = [("lng", 24), ("lnb", 24), ("ng", 4), ("slg", 4), ("slb", 4)]


def columns(table):
    at, out = 0, {}
    for name, n in table:
        out[name] = at
        at += n
    return out, at


CCOL, CN = columns(CONSTS)
PCOL, PN = columns(PARAMS1)
QCOL, QN = columns(PARAMS2)


def build(nc, a, out):
    ctx = ExitStack()
    sem_names = ["slab_used", "bank_full", "free_dve", "free_act", "act_ready", "pe_phase", "act_phase",
                 "dve_phase", "pool_phase", "pe_step", "act_step", "dve_step", "pool_step",
                 "consts_in", "layer_in", "x_in", "store",
                 "ada_full", "ada_copied"]
    settled_names = [n + "_settled" for n in ("pe", "act", "dve", "pool")]
    with ctx:
        S = {n: ctx.enter_context(nc.semaphore(n)) for n in sem_names + settled_names}
        slab_loaded = [ctx.enter_context(nc.semaphore(f"slab_loaded{i}")) for i in range(RING)]
        wk = {n: [ctx.enter_context(nc.semaphore(f"wkv_{n}{d}")) for d in range(2)]
              for n in ("pe", "act", "dve", "pool")}
        arena = ctx.enter_context(nc.sbuf_tensor("arena", [P, 53200], F32))
        bank = [ctx.enter_context(nc.psum_tensor(f"bank{i}", [P, 512], F32)) for i in range(8)]

        def view(at, *dims):
            n = int(np.prod(dims))
            assert at + n <= 53200
            v = arena[:, at:at + n]
            if len(dims) == 1:
                return v
            names = "abcd"[:len(dims)]
            pat = "p (" + " ".join(names) + ") -> p " + " ".join(names)
            return v.rearrange(pat, **{k: d for k, d in zip(names[1:], dims[1:])})

        X0, H0, R0, U0 = 0, 4096, 8192, 24576
        M0, G0 = U0 + 15 * 512, U0 + 15 * 512 + 4096
        C0 = G0 + RING * SLOT
        K0 = C0 + CN
        K1 = K0 + 2 * PN + 8 + 2 * QN + 8
        MOD0 = K1
        SM0 = MOD0 + 2 * 96 + 64 + 16
        CH0 = SM0 + 192
        X = view(X0, KD, 2, T)
        H = view(H0, KD, 2, T)
        cst = arena[:, C0:C0 + CN]

        def con(name, *dims):
            return view(C0 + CCOL[name], *dims)

        ident, ones, blk64 = con("ident", P), con("ones", P), con("blk64", P)
        cum = con("cum", 2, 2, P)
        m1 = con("m1", 2, P)
        inv = con("inv", 2, LEVELS, C)
        neg0 = con("neg0", 2, 2, C)
        eye64 = con("eye64", C)
        tril = con("tril", P)
        pick = con("pick", 2)

        def par(l, name, *dims):
            return view(K0 + l * PN + PCOL[name], *dims)

        final_g = view(K0 + 2 * PN, 8)
        P2 = K0 + 2 * PN + 8

        def par2(name, n):
            return arena[:, P2:P2 + 2 * QN].rearrange("p (l n) -> p l n", l=2)[:, :, QCOL[name]:QCOL[name] + n]

        hg_lb = view(P2 + 2 * QN, 2, 4)
        MOD = [view(MOD0 + 96 * l, 48, 2) for l in range(2)]
        GS = [view(MOD0 + 192 + 16 * n, KD, 2) for n in range(4)]
        cond = view(MOD0 + 256, KD, 2)
        FS = view(SM0, 2, 4, NCH)
        DM = view(SM0 + 64, 2, 4, NCH)
        DE = view(SM0 + 128, 2, 4, NCH)

        class Eng:

            def __init__(self, eng, name):
                self.e, self.name = eng, name
                self.c = {n: 0 for n in sem_names}
                self.wk = 0
                self.slab = 0
                self.l = None

            def v(self, name, n):
                x = self.c[name] + n
                return x if self.l is None else x + self.l * PER[name]

        def settled(E):
            E.e.sem_inc(S[E.name + "_settled"], 1)

        def phase(E):
            E.e.drain().then_inc(S[E.name + "_phase"], 1)
            for o in ("pe", "act", "dve", "pool"):
                E.c[o + "_phase"] += 1
                if o != E.name:
                    E.e.wait_ge(S[o + "_phase"], E.v(o + "_phase", 0))
            if E.l is not None:
                settled(E)

        def repeat(E, n, body, fn):
            if n // body > 1:
                with E.e.Fori(0, n // body) as i:
                    fn(i, body)
            elif n // body == 1:
                fn(0, body)
            if n % body:
                fn(n // body, n % body)

        def slab_to_slot(E, s, i, body, src, w):
            k = E.slab + s
            n = i * body + (k + 1)
            E.e.wait_ge(S["slab_used"], n if E.l is None else E.l * SLABS2 + n)
            slot = (k if not isinstance(i, int) else k + i * body) % RING
            E.e.dma_start(view(G0 + slot * SLOT, w), src).then_inc(slab_loaded[slot], 16)

        def load_slabs(E, src, n, tiles, body=4, first=0):
            w = tiles * P

            def some(i, count):
                for s in range(count):
                    slab_to_slot(E, s, i, body, src(i * body + s + first), w)

            repeat(E, n, body, some)
            E.slab += n

        def slab_wait(E, s, i, body):
            k = E.slab + s
            val = 16 * (k // RING + 1)
            if not isinstance(i, int):
                val = i * (16 * body // RING) + val
            else:
                val = 16 * ((k + i * body) // RING + 1)
            if E.l is not None:
                val = E.l * (16 * SLABS2 // RING) + val
            slot = (k if not isinstance(i, int) else k + i * body) % RING
            E.e.wait_ge(slab_loaded[slot], val)
            return view(G0 + slot * SLOT, 11, P)

        def gemm_pe(E, units, K, tiles, rhs, N, free, body=4, ready=None):
            per = body * K // tiles
            assert units <= body or (per % RING == 0 and body % 4 == 0 and body * K % tiles == 0)

            def some(i, count, first=False):
                t = 0
                for u in range(count):
                    E.e.wait_ge(S[free], E.v(free, i * body + u + 1))
                    for k in range(K):
                        if t % tiles == 0:
                            w = slab_wait(E, t // tiles, i, per)
                        if first and u == 0:
                            E.e.wait_ge(S[ready[0]], E.v(ready[0], ready[1](k)))
                            settled(E)
                        mm = E.e.matmul(bank[u % 4][:, 0:N], w[:, t % tiles, :], rhs(k), start=(k == 0), stop=(k == K - 1))
                        if t % tiles == 0:
                            mm.then_inc(S["slab_used"], 1)
                        t += 1
                    mm.then_inc(S["bank_full"], 1)

            if ready:
                some(0, body, True)
                if units == 2 * body:
                    some(1, body)
                elif units > body:
                    with E.e.Fori(1, units // body) as i:
                        some(i, body)
            else:
                repeat(E, units, body, some)
            E.slab += units * K // tiles

        def units_done(E, n, free, pairs=0):
            E.c["bank_full"] += n
            E.c[free] += n
            E.c["act_ready"] += pairs

        def gated_act(E, n, func, N, tmp):
            def some(i, count):
                for q in range(count // 2):
                    E.e.wait_ge(S["bank_full"], E.v("bank_full", i * 4 + 2 * q + 1))
                    E.e.wait_ge(S["free_dve"], E.v("free_dve", i * 4 + 2 * q + 2))
                    E.e.activation(tmp[:, q % 2, 0:N], bank[2 * q][:, 0:N], func).then_inc(S["act_ready"], 1)
            repeat(E, n, 4, some)

        def gated_dve(E, n, dst, N, tmp):
            def some(i, count):
                for q in range(count // 2):
                    E.e.wait_ge(S["act_ready"], E.v("act_ready", i * 2 + q + 1))
                    E.e.wait_ge(S["bank_full"], E.v("bank_full", i * 4 + 2 * q + 2))
                    E.e.tensor_tensor(dst(i * 2 + q), tmp[:, q % 2, 0:N], bank[2 * q + 1][:, 0:N],
                                      ALU.mult).then_inc(S["free_dve"], 2)
            repeat(E, n, 4, some)

        def take_units(E, free, n, fn, body=4):
            def some(i, count):
                for u in range(count):
                    E.e.wait_ge(S["bank_full"], E.v("bank_full", i * body + u + 1))
                    fn(i * body + u, bank[u % 4]).then_inc(S[free], 1)
            repeat(E, n, body, some)

        def steps(E, pe=0, act=0, dve=0, pool=0):
            for k, n in (("pe", pe), ("act", act), ("dve", dve), ("pool", pool)):
                E.c[k + "_step"] += n

        def one(n):
            return slice(n, n + 1) if isinstance(n, int) else bass.ds(n, 1)

        def cols(at, n):
            return slice(at, at + n) if isinstance(at, int) else bass.ds(at, n)

        XF = view(X0, KD, 2 * T)
        HF = view(H0, KD, 2 * T)
        MIXF = view(M0, KD, 2 * T)

        def rstd_dve(E, pairs, inv_n, eps):
            for src, dst in pairs:
                E.e.tensor_scalar(dst, src, inv_n, eps, ALU.mult, ALU.add)
            E.e.drain()
            for src, dst in pairs:
                E.e.reciprocal(dst, dst).then_inc(S["dve_step"], 1)

        def rms_factor(E, N, after_units=True):
            rs = view(CH0, 2 * T)
            if E.name == "act":
                for k in range(KD):
                    if after_units:
                        E.e.wait_ge(S["free_dve"], E.v("free_dve", k - 3))
                    E.e.activation(HF[:, k, 0:N], XF[:, k, 0:N], ACT.Square).then_inc(S["act_step"], 1)
                E.e.wait_ge(S["dve_step"], E.v("dve_step", 1))
                E.e.activation(rs[:, 0:N], rs[:, 0:N], ACT.Sqrt).then_inc(S["act_step"], 1)
            if E.name == "pe":
                for k in range(KD):
                    E.e.wait_ge(S["act_step"], E.v("act_step", k + 1))
                    mm = E.e.matmul(bank[4][:, 0:N], ones, HF[:, k, 0:N], start=(k == 0), stop=(k == KD - 1))
                mm.then_inc(S["pe_step"], 1)
            if E.name == "dve":
                E.e.wait_ge(S["pe_step"], E.v("pe_step", 1))
                rstd_dve(E, [(bank[4][:, 0:N], rs[:, 0:N])], 1.0 / D, RMS_EPS)
            steps(E, pe=1, act=KD + 1, dve=1)

        def rms_apply(E, N, gs, shift, dst):
            rs = view(CH0, 2 * T)
            if E.name == "act" and shift is not None:
                for k in range(KD):
                    E.e.wait_ge(S["dve_step"], E.v("dve_step", 1 + k))
                    for s in range(N // T):
                        ins = E.e.activation(dst[:, k, s * T:(s + 1) * T], dst[:, k, s * T:(s + 1) * T],
                                             ACT.Identity, bias=shift(k, s))
                    ins.then_inc(S["act_step"], 1)
            if E.name == "dve":
                E.e.wait_ge(S["act_step"], E.v("act_step", 0))
                for k in range(KD):
                    for s in range(N // T):
                        ins = E.e.scalar_tensor_tensor(out=dst[:, k, s * T:(s + 1) * T], in0=XF[:, k, s * T:(s + 1) * T],
                                                       scalar=gs(k, s), in1=rs[:, s * T:(s + 1) * T],
                                                       op0=ALU.mult, op1=ALU.mult)
                    ins.then_inc(S["dve_step"], 1)
            steps(E, dve=KD)
            if shift is not None:
                steps(E, act=KD)
            else:
                phase(E)

        def rms(E, N, gs, shift, dst):
            rms_factor(E, N)
            rms_apply(E, N, gs, shift, dst)

        def layer_norm(E, src, dst, K, gain, shift, scr):
            cen, sq, rs = view(scr, K, T), view(scr + K * T, K, T), view(scr + 2 * K * T, T)
            if E.name == "pe":
                for k in range(K):
                    E.e.wait_ge(S["free_dve"], E.v("free_dve", k - K + 5))
                    mm = E.e.matmul(bank[4][:, 0:T], ones, src(k), start=(k == 0), stop=(k == K - 1))
                mm.then_inc(S["pe_step"], 1)
                for k in range(K):
                    E.e.wait_ge(S["act_step"], E.v("act_step", k + 1))
                    mm = E.e.matmul(bank[5][:, 0:T], ones, sq[:, k, :], start=(k == 0), stop=(k == K - 1))
                mm.then_inc(S["pe_step"], 1)
            if E.name == "dve":
                E.e.wait_ge(S["pe_step"], E.v("pe_step", 1))
                for k in range(K):
                    E.e.scalar_tensor_tensor(out=cen[:, k, :], in0=bank[4][:, 0:T], scalar=-1.0 / (K * P),
                                                     in1=src(k), op0=ALU.mult, op1=ALU.add).then_inc(S["dve_step"], 1)
                E.e.wait_ge(S["pe_step"], E.v("pe_step", 2))
                rstd_dve(E, [(bank[5][:, 0:T], rs)], 1.0 / (K * P), LN_EPS)
                E.e.wait_ge(S["act_step"], E.v("act_step", K + 1))
                for k in range(K):
                    E.e.scalar_tensor_tensor(out=dst(k), in0=cen[:, k, :], scalar=gain(k), in1=rs,
                                                     op0=ALU.mult, op1=ALU.mult).then_inc(S["dve_step"], 1)
            if E.name == "act":
                for k in range(K):
                    E.e.wait_ge(S["dve_step"], E.v("dve_step", k + 1))
                    E.e.activation(sq[:, k, :], cen[:, k, :], ACT.Square).then_inc(S["act_step"], 1)
                E.e.wait_ge(S["dve_step"], E.v("dve_step", K + 1))
                E.e.activation(rs, rs, ACT.Sqrt).then_inc(S["act_step"], 1)
                for k in range(K):
                    E.e.wait_ge(S["dve_step"], E.v("dve_step", K + 2 + k))
                    E.e.activation(dst(k), dst(k), ACT.Identity, bias=shift(k)).then_inc(S["act_step"], 1)
            steps(E, pe=2, act=2 * K + 1, dve=2 * K + 1)

        def column_major(ap):
            return ap.rearrange("p (r c) -> p c r", r=4)

        def by_four(ap):
            return ap.rearrange("p (c r) -> p c r", r=4)

        US = view(U0, 15, 2 * T)
        Z = view(R0, 4, 2, ZW)
        QK = view(R0, 8, 2, 2 * T)
        KB = view(R0 + 8192, 8, 2, 2 * T)
        ADA_FIRST = 27

        silu_c = view(CH0 + 2560, KD, 32)
        ada_rows = view(CH0 + 2816, 2, 3 * P)

        def ada_sum(E, u, q, s, i, per):
            w = slab_wait(E, s, i, per)
            for k in range(KD):
                r = 32 * (k % 4)
                mm = E.e.matmul(bank[5 + u % 2][r:r + 32, q * P:(q + 1) * P], silu_c[:, k, :], w[:, k, :],
                                start=(k < 4), stop=(k >= 4), skip_group_check=True)
                if k == 0:
                    mm.then_inc(S["slab_used"], 1)
            if q == 2:
                mm.then_inc(S["ada_full"], 1)

        def ada_turn(E, u, n, chunk):
            E.e.wait_ge(S["ada_copied"], E.v("ada_copied", n + 1))
            for q in range(3):
                E.e.matmul(bank[7][:, cols((chunk + q) * 2, 2)], ada_rows[:, u % 2, q * P:(q + 1) * P], pick,
                           start=True, stop=True)

        def ada_copy(E, u, n):
            E.e.wait_ge(S["ada_full"], E.v("ada_full", n + 1))
            E.e.activation(ada_rows[:, u % 2, :], bank[5 + u % 2][:, 0:3 * P], ACT.Copy).then_inc(S["ada_copied"], 1)

        def trios_done(E, n):
            E.c["ada_full"] += n
            E.c["ada_copied"] += n

        def modulation_start(E):
            if E.name == "dve":
                E.e.memset(silu_c, 0.0).then_inc(S["dve_step"], 1)
            if E.name == "act":
                E.e.wait_ge(S["dve_step"], E.v("dve_step", 1))
                E.e.activation(silu_c[:, :, 0:2], cond, ACT.Silu).then_inc(S["act_step"], 1)
            if E.name == "pe":
                E.e.wait_ge(S["act_step"], E.v("act_step", 1))
            steps(E, act=1, dve=1)
            rms_factor(E, 2 * T, False)
            if E.name == "act":
                def some(i, count):
                    for u in range(count):
                        ada_copy(E, u, i * 4 + u)
                repeat(E, ADA_FIRST // 3, 4, some)
            if E.name == "pe":
                def some(i, count):
                    for u in range(count):
                        for q in range(3):
                            ada_sum(E, u, q, 3 * u + q, i, 12)
                        if u:
                            ada_turn(E, u - 1, i * 4 + (u - 1), i * 12 + 3 * (u - 1))
                    ada_turn(E, count - 1, i * 4 + (count - 1), i * 12 + 3 * (count - 1))
                repeat(E, ADA_FIRST // 3, 4, some)
                E.slab += ADA_FIRST
            trios_done(E, ADA_FIRST // 3)
            phase(E)
            if E.name == "dve":
                modulation_out(E, 0, 0, 16)
                norm_gain(E, 0, 0)
            phase(E)

        def modulation_out(E, l, m0, m1_):
            b = bank[7][:, 96 * l + 2 * m0:96 * l + 2 * m1_].rearrange("p (m s) -> p m s", s=2)
            E.e.tensor_tensor(MOD[l][:, m0:m1_, :], b,
                              par(l, "adab", 48, 1)[:, m0:m1_, :].broadcast_to([P, m1_ - m0, 2]), ALU.add)
            E.e.drain()

        def norm_gain(E, l, n):
            g = GS[2 * l + n]
            E.e.tensor_scalar(g, MOD[l][:, 24 * n + 8:24 * n + 16, :], 1.0, None, ALU.add)
            E.e.drain()
            E.e.tensor_tensor(g, g, par(l, "n1g" if n == 0 else "n2g", 8, 1).broadcast_to([P, 8, 2]), ALU.mult)

        def input_projection(E, l):
            Nc = 2 * T if l == 0 else T
            S_ = Nc // T
            side = 3 if l == 0 else 0
            tmp = view(CH0, 2, 512)
            raw = view(CH0 + 1024, 2, 2, T + 2)
            if E.name == "pe":
                E.e.wait_ge(S["act_step"], E.v("act_step", 0))
                for units, N, chunk0 in ((8, Nc, ADA_FIRST), (15, 2 * T, ADA_FIRST + 24)):
                    slabs_each = 5 if side else 1
                    per = 4 * slabs_each

                    def turn(i, u):
                        ada_turn(E, u, i * 4 + u, i * 12 + (chunk0 + 3 * u))

                    def some(i, count):
                        for u in range(count):
                            E.e.wait_ge(S["free_dve"], E.v("free_dve", i * 4 + u + 1))
                            s = u * slabs_each
                            w = slab_wait(E, s, i, per)
                            for k in range(KD):
                                if side and k == 4:
                                    ada_sum(E, u, 0, s + 1, i, per)
                                    w = slab_wait(E, s + 2, i, per)
                                mm = E.e.matmul(bank[u % 4][:, 0:N], w[:, k % 4 if side else k, :], HF[:, k, 0:N],
                                                start=(k == 0), stop=(k == KD - 1))
                                if k == 0 or side and k == 4:
                                    mm.then_inc(S["slab_used"], 1)
                            mm.then_inc(S["bank_full"], 1)
                            if side:
                                if u:
                                    turn(i, u - 1)
                                ada_sum(E, u, 1, s + 3, i, per)
                                ada_sum(E, u, 2, s + 4, i, per)
                        if side:
                            turn(i, count - 1)
                    repeat(E, units, 4, some)
                    E.slab += units * slabs_each
                    units_done(E, units, "free_dve")
                    if side:
                        trios_done(E, units)
            else:
                if E.name == "act":
                    def some(i, count):
                        for q in range(2):
                            E.e.wait_ge(S["bank_full"], E.v("bank_full", i * 4 + 2 * q + 1))
                            E.e.wait_ge(S["free_dve"], E.v("free_dve", i * 4 + 2 * q + 2))
                            E.e.activation(tmp[:, q % 2, 0:Nc], bank[2 * q][:, 0:Nc], ACT.Sigmoid).then_inc(S["act_ready"], 1)
                            if side:
                                ada_copy(E, 2 * q, i * 4 + 2 * q)
                                ada_copy(E, 2 * q + 1, i * 4 + (2 * q + 1))
                    repeat(E, 8, 4, some)
                if E.name == "dve":
                    E.e.memset(Z, 0.0)
                    E.e.memset(raw, 0.0)
                    E.e.drain()

                    def some(i, count):
                        for q in range(2):
                            E.e.wait_ge(S["act_ready"], E.v("act_ready", i * 2 + q + 1))
                            E.e.wait_ge(S["bank_full"], E.v("bank_full", i * 4 + 2 * q + 2))
                            for s in range(S_):
                                o = Z[:, one(i * 2 + q), s, PAD:PAD + T].rearrange("p o t -> p (o t)")
                                i0, i1 = tmp[:, q, s * T:(s + 1) * T], bank[2 * q + 1][:, s * T:(s + 1) * T]
                                if l == 1:
                                    o, i0, i1 = by_four(o), column_major(i0), column_major(i1)
                                ins = E.e.tensor_tensor(o, i0, i1, ALU.mult)
                            ins.then_inc(S["free_dve"], 2)
                    repeat(E, 8, 4, some)
                    E.e.drain()
                units_done(E, 8, "free_dve", 4)
                if side:
                    trios_done(E, 8)
                if E.name == "act":
                    def some(i, count):
                        for u in range(count):
                            E.e.wait_ge(S["bank_full"], E.v("bank_full", i * 4 + u + 1))
                            E.e.wait_ge(S["free_dve"], E.v("free_dve", i * 4 + u + 3))
                            src = bank[u % 4][:, :].rearrange("p (s t) -> p s t", t=T)
                            if l == 0:
                                ins = E.e.activation(raw[:, u % 2, :, 1:T + 1], src, ACT.Copy)
                            else:
                                E.e.activation(by_four(raw[:, u % 2, 0, 1:T + 1]), column_major(src[:, 0, :]), ACT.Copy)
                                ins = E.e.activation(raw[:, u % 2, 1, 1:T + 1], src[:, 1, :], ACT.Copy)
                            ins.then_inc(S["act_ready"], 1)
                            if side:
                                ada_copy(E, u, i * 4 + u)
                    repeat(E, 15, 4, some)
                if E.name == "dve":
                    sw, cw, cb = par(l, "sw", 15, 3), par(l, "cw", 4, CONV_K), par(l, "cb", 4)

                    def wide(t, first=False):
                        for k in range(4):
                            o = MIXF[:, k, 0:Nc].rearrange("p (s t) -> p s t", t=T)
                            z = Z[:, k, 0:S_, cols(t, T)]
                            if first:
                                E.e.tensor_scalar(o, z, cw[:, k, 0:1], cb[:, k:k + 1], ALU.mult, ALU.add)
                            else:
                                E.e.scalar_tensor_tensor(out=o, in0=z, scalar=cw[:, k, one(t)], in1=o,
                                                         op0=ALU.mult, op1=ALU.add)
                        E.e.drain()

                    wide(0, True)

                    def some(i, count):
                        for u in range(count):
                            n = i * 2 + u
                            E.e.wait_ge(S["act_ready"], E.v("act_ready", n + 1))
                            o = US[:, one(n), :].rearrange("p o (s t) -> p (o s) t", t=T)
                            E.e.tensor_scalar(o, raw[:, u, :, 1:T + 1], sw[:, one(n), 1], None, ALU.mult)
                            for tap in (0, 2):
                                E.e.drain()
                                ins = E.e.scalar_tensor_tensor(out=o, in0=raw[:, u, :, tap:tap + T],
                                                               scalar=sw[:, one(n), tap], in1=o, op0=ALU.mult, op1=ALU.add)
                            ins.then_inc(S["free_dve"], 1)
                            wide(n * 2 + 1)
                            wide(n * 2 + 2)
                    repeat(E, 15, 2, some)
                units_done(E, 15, "free_dve", 15)
                if side:
                    trios_done(E, 15)
            if E.name == "pe":
                E.c["act_ready"] += 19
            phase(E)

        SIG = view(H0, 8, 512)
        DU, IU = view(M0 + 2048, 1024), view(M0 + 3072, 1024)
        GU = view(CH0, 2, 512)
        WL = view(CH0 + 1024, 512)
        KKN = view(CH0 + 1536, 4, 512)
        NR = view(CH0 + 3584, 4, 512)
        AR = view(CH0 + 5632, 2, 512)
        EN = view(CH0 + 6656, 2, 512)

        def rwkv_prep(E, l):
            ka = par(l, "ka", 4)
            if E.name == "act":
                for dst, src in ((DU[0:65, :], a["decay_w"][l]), (IU[64:128, :], a["iclr_w"][l]), (GU, a["gate_w"][l])):
                    E.e.dma_start(dst, src).then_inc(S["layer_in"], 16)
                E.e.activation(WL[0:64, :], US[0:64, 12, :], ACT.Tanh).then_inc(S["act_step"], 1)
                E.e.activation(US[:, 13, :], US[:, 13, :], ACT.Sigmoid)
                E.e.activation(US[0:32, 14, :], US[0:32, 14, :], ACT.Sigmoid)
                for p in range(4):
                    E.e.wait_ge(S["pe_step"], E.v("pe_step", p + 1))
                    E.e.activation(NR[:, p, :], bank[p][:, :], ACT.Sqrt).then_inc(S["act_step"], 1)
                for g in range(8):
                    E.e.wait_ge(S["pe_step"], E.v("pe_step", 5 + g))
                    E.e.activation(SIG[:, g, :], bank[(4 + g) % 8][:, :], ACT.Sigmoid).then_inc(S["act_step"], 1)
                for g in range(8):
                    E.e.wait_ge(S["pe_step"], E.v("pe_step", 13 + g))
                    E.e.activation(KB[:, g, 1, :], bank[4 + g % 4][:, :], ACT.Sigmoid,
                                   bias=par(l, "ib0", 8)[:, g:g + 1]).then_inc(S["act_step"], 1)
                for g in range(8):
                    d, p = divmod(g, 4)
                    E.e.wait_ge(S["pe_step"], E.v("pe_step", 21 + g))
                    if g >= 2:
                        E.e.wait_ge(S["dve_step"], E.v("dve_step", 5 + g))
                    A, B = bank[2 * (g % 2)][:, :], bank[2 * (g % 2) + 1][:, :]
                    first, last = (0, C - 1) if d == 0 else (C - 1, 0)
                    E.e.activation(EN[:, g % 2, :], A, ACT.Exp, scale=KAPPA)
                    E.e.activation(QK[:, g, 1, :], A, ACT.Exp, scale=-KAPPA)
                    E.e.activation(QK[:, g, 0, :], B, ACT.Exp, scale=-KAPPA)
                    E.e.activation(DE[:, d, p, :], A[:, last::C], ACT.Exp, scale=-KAPPA)
                    E.e.activation(DM[:, d, p, :], B[:, first::C], ACT.Exp, scale=KAPPA).then_inc(S["act_step"], 1)
            if E.name == "pe":
                for p in range(4):
                    E.e.wait_ge(S["dve_step"], E.v("dve_step", p + 1))
                    E.e.matmul(bank[p][:, :], blk64, NR[:, p, :], start=True, stop=True).then_inc(S["pe_step"], 1)
                E.e.wait_ge(S["layer_in"], E.v("layer_in", 48))
                E.e.wait_ge(S["act_step"], E.v("act_step", 1))
                E.e.wait_ge(S["dve_step"], E.v("dve_step", 5))
                for g in range(8):
                    d, j = divmod(g, 4)
                    if g >= 4:
                        E.e.wait_ge(S["act_step"], E.v("act_step", g - 2))
                    E.e.matmul(bank[(4 + g) % 8][:, :], WL[0:65, j * P:(j + 1) * P], DU[0:65, d * 512:(d + 1) * 512],
                               start=True, stop=True).then_inc(S["pe_step"], 1)
                for g in range(8):
                    E.e.wait_ge(S["act_step"], E.v("act_step", 6 + g if g < 4 else 10 + g))
                    E.e.matmul(bank[4 + g % 4][:, :], IU[64:128, g * P:(g + 1) * P],
                               US[64:128, 12, :], start=True, stop=True).then_inc(S["pe_step"], 1)
                for g in range(8):
                    d, p = divmod(g, 4)
                    E.e.wait_ge(S["act_step"], E.v("act_step", 13 if g < 2 else 20 + g))
                    for x in range(2):
                        for j in range(4):
                            mm = E.e.matmul(bank[2 * (g % 2) + x][:, j * P:(j + 1) * P], SIG[:, d * 4 + j, p * P:(p + 1) * P],
                                            cum[:, d, x, :], start=True, stop=True)
                    mm.then_inc(S["pe_step"], 1)
                    if g % 2:
                        q = g // 2
                        if g == 1:
                            E.e.wait_ge(S["act_step"], E.v("act_step", 21))
                        E.e.matmul(bank[4 + q][:, :], GU[:, 0, q * P:(q + 1) * P], US[:, 13, :], start=True, stop=False)
                        E.e.matmul(bank[4 + q][:, :], GU[0:32, 1, q * P:(q + 1) * P], US[0:32, 14, :], start=False, stop=True)
            if E.name == "pool":
                E.e.wait_ge(S["dve_step"], E.v("dve_step", 6))
                for g in range(8):
                    E.e.wait_ge(S["act_step"], E.v("act_step", 22 + g))
                    E.e.tensor_tensor(QK[:, g, 1, :], QK[:, g, 1, :], US[:, g % 4, :], ALU.mult)
                    E.e.tensor_tensor(QK[:, g, 0, :], QK[:, g, 0, :], KKN[:, g % 4, :], ALU.mult)
            if E.name == "dve":
                for p in range(4):
                    E.e.tensor_scalar(KKN[:, p, :], US[:, 4 + p, :], par(l, "kk", 4)[:, p:p + 1], None, ALU.mult)
                E.e.drain()
                for p in range(4):
                    E.e.tensor_tensor(NR[:, p, :], KKN[:, p, :], KKN[:, p, :], ALU.mult).then_inc(S["dve_step"], 1)
                if l == 0:
                    modulation_out(E, 0, 16, 48)
                    modulation_out(E, 1, 0, 48)
                    for n in ((0, 1), (1, 0), (1, 1)):
                        norm_gain(E, *n)
                E.e.memset(WL[64:65, :], 1.0).then_inc(S["dve_step"], 1)
                for p in range(4):
                    E.e.wait_ge(S["act_step"], E.v("act_step", 2 + p))
                    E.e.tensor_scalar(NR[:, p, :], NR[:, p, :], 1e-12, None, ALU.max)
                E.e.drain()
                for p in range(4):
                    E.e.reciprocal(NR[:, p, :], NR[:, p, :])
                E.e.drain()
                for p in range(4):
                    E.e.tensor_tensor(KKN[:, p, :], KKN[:, p, :], NR[:, p, :], ALU.mult)
                E.e.drain().then_inc(S["dve_step"], 1)
                for g in range(8):
                    p = g % 4
                    if g == 0:
                        E.e.wait_ge(S["act_step"], E.v("act_step", 21))
                    kd, ar, en = NR[:, g % 2, :], KB[:, g, 1, :], EN[:, g % 2, :]
                    E.e.tensor_scalar(kd, ar, -1.0, ka[:, p:p + 1], ALU.add, ALU.mult)
                    E.e.drain()
                    E.e.scalar_tensor_tensor(out=kd, in0=kd, scalar=1.0, in1=US[:, 4 + p, :], op0=ALU.add, op1=ALU.mult)
                    E.e.tensor_tensor(ar, ar, KKN[:, p, :], ALU.mult)
                    E.e.drain()
                    E.e.wait_ge(S["act_step"], E.v("act_step", 22 + g))
                    E.e.tensor_tensor(KB[:, g, 0, :], kd, en, ALU.mult)
                    E.e.tensor_tensor(ar, ar, en, ALU.mult).then_inc(S["dve_step"], 1)
            E.c["layer_in"] += 48
            steps(E, pe=28, act=29, dve=14)
            phase(E)
            if E.name == "dve":
                for f0, c0, c1, n in ((0, 4, 5, 3), (3, 7, 0, 1), (4, 0, 1, 3)):
                    E.e.tensor_tensor(FS[:, 0, :, f0:f0 + n], DE[:, 0, :, c0:c0 + n], DM[:, 0, :, c1:c1 + n], ALU.mult)
                E.e.tensor_tensor(FS[:, 1, :, 1:8], DE[:, 1, :, 1:8], DM[:, 1, :, 0:7], ALU.mult)
                E.e.memset(FS[:, 0, :, 7:8], 1.0)
                E.e.memset(FS[:, 1, :, 0:1], 1.0)
                for p in range(4):
                    E.e.scalar_tensor_tensor(out=NR[:, p, :], in0=US[:, p, :], scalar=par(l, "rk", 4)[:, p:p + 1],
                                                     in1=US[:, 4 + p, :], op0=ALU.mult, op1=ALU.mult).then_inc(S["dve_step"], 1)
                for p in range(4):
                    E.e.wait_ge(S["pe_step"], E.v("pe_step", p + 1))
                    E.e.tensor_tensor(US[:, p, :], bank[p][:, :], US[:, 8 + p, :], ALU.mult)
            if E.name == "pe":
                for p in range(4):
                    E.e.wait_ge(S["dve_step"], E.v("dve_step", p + 1))
                    E.e.matmul(bank[p][:, :], blk64, NR[:, p, :], start=True, stop=True).then_inc(S["pe_step"], 1)
            if E.name == "act":
                for p in range(4):
                    E.e.wait_ge(S["dve_step"], E.v("dve_step", p + 1))
                    E.e.activation(US[:, 4 + p, :], bank[4 + p][:, :], ACT.Copy)
            steps(E, pe=4, dve=4)
            phase(E)

        def both(at, *dims):
            n = int(np.prod(dims))
            return [view(at + d * n, *dims) for d in range(2)]

        Gm = both(H0 + 2048, 2, 4, P)
        LB = both(U0 + 12 * 512, 4, 2, C)
        AM = [view(U0 + 14 * 512, 2, 4, C), view(CH0, 2, 4, C)]
        QC = both(CH0 + 512, 4, 2, C)
        VC = both(CH0 + 1536, 4, C)
        LT = both(CH0 + 2048, 4, P)
        UV = both(CH0 + 3072, 4, 2, C)
        AN = both(CH0 + 4096, 2, 4, C)
        TN = both(CH0 + 5120, 2, 4, C)
        P1 = both(CH0 + 6144, 4, C)
        XN = both(CH0 + 6656, 4, C)
        ST = both(CH0 + 7168, 4, C)
        YD = [view(M0 + 2048, 4, 2 * T), view(H0, 4, 2 * T)]
        PE_A, PE_T, PE_G, PE_V, PE_L, PE_X, PE_U, PE_Y, PE_D = 1, 2, 3, 4, 4, 15, 16, 17, 18
        ACT_T, ACT_A, ACT_V, ACT_L, ACT_X, ACT_Y = 2, 3, 4, 4, 10, 11
        DVE_T, DVE_G, DVE_L, DVE_U, DVE_S = 1, 2, 2, 8, 9
        POOL_C, POOL_R, POOL_L = 1, 2, 2
        NM = {"pe": 18, "act": 11, "dve": 9, "pool": 7}

        def recurrence(E, emit_context):
            base = E.wk

            def at(who, n, m, back=0):
                w = NM[who]
                return n * w + (w * (base + 1 - back) + m)

            if E.wk == 0:
                for d in range(2):
                    E.e.drain().then_inc(wk[E.name][d], NM[E.name])
            if E.name == "pool":
                for d in range(2):
                    E.e.memset(ST[d], 0.0)
            phase(E)

            tiles = [(p, h) for p in range(4) for h in range(2)]

            def rows(h):
                return slice(h * C, (h + 1) * C)

            def quad(b, at=0):
                return b[:, at:at + 4 * C].rearrange("p (a c) -> p a c", a=4)

            def chunk(n, o, emit=True):
                if E.name == "pool":
                    for d in range(2):
                        E.e.wait_ge(wk["pe"][d], at("pe", n, PE_V, 1))
                        gs = slice(4 * d, 4 * d + 4)
                        oo = cols(o[d], C)
                        E.e.tensor_copy(LB[d][0:C], KB[0:C, gs, :, oo])
                        E.e.drain()
                        E.e.tensor_copy(LB[d][C:P, :, 0, :], KB[C:P, gs, 1, oo])
                        E.e.tensor_copy(LB[d][C:P, :, 1, :], KB[C:P, gs, 0, oo])
                        E.e.drain()
                        E.e.tensor_copy(VC[d], US[:, 8:12, oo])
                    for x, used in ((0, PE_X), (1, PE_Y)):
                        for d in range(2):
                            E.e.wait_ge(wk["pe"][d], at("pe", n, used, 1))
                            gs = slice(4 * d, 4 * d + 4)
                            E.e.tensor_copy(QC[d][:, :, x, :], QK[:, gs, x, cols(o[d], C)]).then_inc(wk["pool"][d], 1)
                    for lv in range(1, LEVELS):
                        for d in range(2):
                            E.e.wait_ge(wk["act"][d], at("act", n, ACT_A))
                            if lv >= 3:
                                E.e.wait_ge(wk["pe"][d], at("pe", n, PE_L + 2 * (lv - 2) - 1))
                            E.e.tensor_tensor(AM[d][:, lv % 2], AN[d][:, 0],
                                                      inv[:, d, lv:lv + 1, :].broadcast_to([P, 4, C]), ALU.mult).then_inc(wk["pool"][d], 1)
                if E.name == "pe":
                    for d in range(2):
                        B = bank[4 * d:4 * d + 4]
                        E.e.wait_ge(wk["pool"][d], at("pool", n, POOL_C))
                        E.e.wait_ge(wk["act"][d], at("act", n, ACT_X, 1))
                        settled(E)
                        for p, h in tiles:
                            r = rows(h)
                            mm = E.e.matmul(B[2][rows(1 - h), p * C:(p + 1) * C], QC[d][r, p, 0, :], LB[d][r, p, 1 - h, :],
                                            start=True, stop=True)
                        mm.then_inc(wk["pe"][d], 1)
                        E.e.wait_ge(wk["dve"][d], at("dve", n, DVE_U, 1))
                        settled(E)
                        for p in range(4):
                            mm = E.e.transpose(B[3][:, p * P:(p + 1) * P], LB[d][:, p].rearrange("p a c -> p (a c)"), ident)
                        mm.then_inc(wk["pe"][d], 1)
                        E.e.wait_ge(wk["act"][d], at("act", n, ACT_Y, 1))
                        E.e.wait_ge(wk["dve"][d], at("dve", n, DVE_S, 1))
                        E.e.wait_ge(wk["pool"][d], at("pool", n, POOL_R))
                        settled(E)
                        for p, h in tiles:
                            r = rows(h)
                            mm = E.e.matmul(B[h][:, p * P:(p + 1) * P], LB[d][r, p].rearrange("p a c -> p (a c)"),
                                            QC[d][r, p].rearrange("p a c -> p (a c)"), start=True, stop=True)
                        mm.then_inc(wk["pe"][d], 1)
                    for d in range(2):
                        B = bank[4 * d:4 * d + 4]
                        E.e.wait_ge(wk["act"][d], at("act", n, ACT_T))
                        settled(E)
                        for p, h in tiles:
                            r = rows(h)
                            mm = E.e.matmul(B[3][r, p * C:(p + 1) * C], VC[d][r, p, :], eye64[r, :], start=True, stop=True)
                        mm.then_inc(wk["pe"][d], 1)
                    for lv in range(1, LEVELS):
                        for d in range(2):
                            B = bank[4 * d:4 * d + 4]
                            E.e.wait_ge(wk["pool"][d], at("pool", n, POOL_L + lv))
                            E.e.wait_ge(wk["dve"][d], at("dve", n, DVE_T if lv == 1 else DVE_L + lv - 1))
                            E.e.wait_ge(wk["act"][d], at("act", n, ACT_A if lv == 1 else ACT_L + lv - 1))
                            settled(E)
                            for p, h in tiles:
                                r = rows(h)
                                mm = E.e.matmul(B[2][r, p * C:(p + 1) * C], AM[d][r, lv % 2, p, :], TN[d][r, 1, p, :],
                                                start=True, stop=True)
                            mm.then_inc(wk["pe"][d], 1)
                        for d in range(2):
                            B = bank[4 * d:4 * d + 4]
                            E.e.wait_ge(wk["act"][d], at("act", n, ACT_L + lv))
                            E.e.wait_ge(wk["dve"][d], at("dve", n, DVE_G))
                            settled(E)
                            for p, h in tiles:
                                r = rows(h)
                                mm = E.e.matmul(B[0][r, p * C:(p + 1) * C], P1[d][r, p, :], TN[d][r, 0, p, :],
                                                start=True, stop=True)
                                if lv < LEVELS - 1:
                                    mm = E.e.matmul(B[0][r, (4 + p) * C:(5 + p) * C], TN[d][r, 0, p, :], P1[d][r, p, :],
                                                    start=True, stop=True)
                            mm.then_inc(wk["pe"][d], 1)
                    for d in range(2):
                        B = bank[4 * d:4 * d + 4]
                        E.e.wait_ge(wk["act"][d], at("act", n, ACT_L + LEVELS - 1))
                        E.e.wait_ge(wk["dve"][d], at("dve", n, DVE_S, 1))
                        settled(E)
                        for p, h in tiles:
                            r = rows(h)
                            x_out = B[2][rows(1 - h), p * C:(p + 1) * C]
                            E.e.matmul(x_out, Gm[d][r, h, p, 0:C], UV[d][r, p, h, :], start=True, stop=False)
                            mm = E.e.matmul(x_out, QC[d][r, p, 0, :], ST[d][r, p, :], start=False, stop=True)
                        mm.then_inc(wk["pe"][d], 1)
                    for d in range(2):
                        B = bank[4 * d:4 * d + 4]
                        E.e.wait_ge(wk["act"][d], at("act", n, ACT_X))
                        E.e.wait_ge(wk["dve"][d], at("dve", n, DVE_L + LEVELS - 1))
                        settled(E)
                        for p, h in tiles:
                            mm = E.e.matmul(B[3][rows(1 - h), p * C:(p + 1) * C], TN[d][rows(1 - h), 0, p, :], XN[d][rows(1 - h), p, :],
                                            start=True, stop=True)
                        mm.then_inc(wk["pe"][d], 1)
                    for d in range(2):
                        B = bank[4 * d:4 * d + 4]
                        E.e.wait_ge(wk["dve"][d], at("dve", n, DVE_U))
                        settled(E)
                        for p, h in tiles if emit else ():
                            E.e.matmul(B[0][rows(h), p * C:(p + 1) * C], UV[d][:, p, h, :], Gm[d][:, h, p, C:P],
                                       start=(p == 0), stop=False, skip_group_check=True)
                        for p, h in tiles if emit else ():
                            r = rows(h)
                            mm = E.e.matmul(B[0][r, p * C:(p + 1) * C], ST[d][r, p, :], QC[d][r, p, 1, :],
                                            start=False, stop=True, skip_group_check=True)
                        if emit:
                            mm.then_inc(wk["pe"][d], 1)
                        for p, h in tiles:
                            mm = E.e.matmul(B[1][rows(h), p * C:(p + 1) * C], LT[d][:, p, rows(h)], UV[d][:, p, h, :],
                                            start=True, stop=True)
                        mm.then_inc(wk["pe"][d], 1 if emit else 2)
                if E.name == "act":
                    for d in range(2):
                        B = bank[4 * d:4 * d + 4]
                        E.e.wait_ge(wk["pe"][d], at("pe", n, PE_A))
                        E.e.wait_ge(wk["pool"][d], at("pool", n, POOL_L + LEVELS - 1, 1))
                        E.e.wait_ge(wk["dve"][d], at("dve", n, DVE_T, 1))
                        E.e.activation(AN[d][:, 1], quad(B[2]), ACT.Copy).then_inc(wk["act"][d], 1)
                        E.e.wait_ge(wk["pe"][d], at("pe", n, PE_T))
                        E.e.activation(LT[d], B[3][:, :].rearrange("p (a c) -> p a c", a=4), ACT.Copy).then_inc(wk["act"][d], 1)
                        E.e.wait_ge(wk["pe"][d], at("pe", n, PE_G))
                        E.e.activation(AN[d][C:P, 0], B[0][C:P, :].rearrange("p (a c) -> p a c", a=4)[:, :, 0:C], ACT.Copy)
                        E.e.activation(AN[d][0:C, 0], B[1][0:C, :].rearrange("p (a c) -> p a c", a=4)[:, :, 0:C],
                                       ACT.Copy).then_inc(wk["act"][d], 1)
                    for d in range(2):
                        B = bank[4 * d:4 * d + 4]
                        E.e.wait_ge(wk["pe"][d], at("pe", n, PE_V))
                        E.e.activation(UV[d][0:C, :, 0, :], quad(B[3])[0:C], ACT.Copy)
                        E.e.activation(UV[d][C:P, :, 1, :], quad(B[3])[C:P], ACT.Copy).then_inc(wk["act"][d], 1)
                    for lv in range(1, LEVELS):
                        for d in range(2):
                            E.e.wait_ge(wk["pe"][d], at("pe", n, PE_L + 2 * lv - 1))
                            E.e.activation(P1[d], quad(bank[4 * d + 2]), ACT.Copy, scale=-1.0).then_inc(wk["act"][d], 1)
                    for d in range(2):
                        E.e.wait_ge(wk["pe"][d], at("pe", n, PE_X))
                        E.e.activation(XN[d], quad(bank[4 * d + 2]), ACT.Copy, scale=-1.0).then_inc(wk["act"][d], 1)
                    for d in range(2):
                        if not emit:
                            E.e.drain().then_inc(wk["act"][d], 1)
                            continue
                        E.e.wait_ge(wk["pe"][d], at("pe", n, PE_Y))
                        E.e.activation(YD[d][:, :, cols(o[d], C)], quad(bank[4 * d]), ACT.Copy).then_inc(wk["act"][d], 1)
                if E.name == "dve":
                    for d in range(2):
                        B = bank[4 * d:4 * d + 4]
                        E.e.wait_ge(wk["act"][d], at("act", n, ACT_A))
                        E.e.wait_ge(wk["pe"][d], at("pe", n, PE_U, 1))
                        E.e.tensor_tensor(TN[d], AN[d], neg0[:, d].unsqueeze(2).broadcast_to([P, 2, 4, C]), ALU.mult)
                        E.e.drain()
                        flat = TN[d].rearrange("p x a c -> p (x a) c")
                        E.e.tensor_tensor(flat, flat, eye64.unsqueeze(1).broadcast_to([P, 8, C]), ALU.add).then_inc(wk["dve"][d], 1)
                        E.e.wait_ge(wk["pe"][d], at("pe", n, PE_G))
                        for h in range(2):
                            ins = E.e.tensor_tensor(Gm[d][:, h], B[h][:, :].rearrange("p (a c) -> p a c", a=4),
                                                    m1[:, d:d + 1, :].broadcast_to([P, 4, P]), ALU.mult)
                        ins.then_inc(wk["dve"][d], 1)
                    for lv in range(1, LEVELS):
                        x = 2 if lv < LEVELS - 1 else 1
                        for d in range(2):
                            E.e.wait_ge(wk["pe"][d], at("pe", n, PE_L + 2 * lv))
                            t = TN[d][:, 0:x].rearrange("p x a c -> p (x a c)")
                            E.e.tensor_tensor(t, bank[4 * d][:, 0:x * 4 * C], t, ALU.add).then_inc(wk["dve"][d], 1)
                    for d in range(2):
                        B = bank[4 * d:4 * d + 4]
                        E.e.wait_ge(wk["pe"][d], at("pe", n, PE_U))
                        E.e.tensor_copy(UV[d][C:P, :, 0, :], quad(B[3])[C:P])
                        E.e.tensor_copy(UV[d][0:C, :, 1, :], quad(B[3])[0:C]).then_inc(wk["dve"][d], 1)
                    for d in range(2):
                        E.e.wait_ge(wk["pe"][d], at("pe", n, PE_D))
                        E.e.tensor_tensor(ST[d], ST[d], quad(bank[4 * d + 1]), ALU.add)
                        E.e.drain()
                        turn = n if d == 0 else n * -1 + 7
                        E.e.tensor_tensor(ST[d], ST[d], FS[:, d, :, one(turn)].broadcast_to([P, 4, C]), ALU.mult).then_inc(wk["dve"][d], 1)

            if emit_context:
                with E.e.Fori(0, 2) as seg:
                    with E.e.Fori(0, 4) as j:
                        chunk(seg * 4 + j, (seg * -T + j * C + T, seg * -T + j * -C + (2 * T - C)))
            else:
                with E.e.Fori(0, 4) as j:
                    chunk(j, (j * C + T, j * -C + (2 * T - C)), False)
                with E.e.Fori(0, 4) as j:
                    chunk(j + 4, (j * C, j * -C + (T - C)))
            E.wk += NCH
            phase(E)

        def mix_out(E, l):
            N = 2 * T if l == 0 else T
            cen, sq = view(R0, 8, N), view(R0 + 4096, 8, N)
            var = view(CH0, 2, N)
            gather, spread = view(CH0 + 1024, 32), view(CH0 + 1056, P)
            eps = (LN_EPS, GN_EPS)
            spread_bank = (1, 2, 3, 5, 6, 7, 0, 4)

            def order(ap):
                return ap if l == 0 else column_major(ap)

            def natural(ap):
                return ap if l == 0 else by_four(ap)

            if E.name == "pe":
                for j in range(8):
                    if j >= 4:
                        E.e.wait_ge(S["dve_step"], E.v("dve_step", j - 3))
                    E.e.matmul(bank[j][:, 0:N], blk64, MIXF[:, j, 0:N], start=True, stop=True).then_inc(S["pe_step"], 1)
                E.e.wait_ge(S["layer_in"], E.v("layer_in", 16))
                for half in range(2):
                    for k in range(4):
                        E.e.wait_ge(S["act_step"], E.v("act_step", 4 * half + k + 1))
                        mm = E.e.matmul(bank[4 * half][32 * k:32 * k + 32, 0:N], gather, sq[:, 4 * half + k, :], start=True, stop=True)
                    mm.then_inc(S["pe_step"], 1)
                for j in range(8):
                    r = slice(32 * (j % 4), 32 * (j % 4) + 32)
                    if j % 4 == 0:
                        E.e.wait_ge(S["act_step"], E.v("act_step", 9 + j // 4))
                    E.e.matmul(bank[spread_bank[j]][:, 0:N], spread[r, :], var[r, j // 4, :],
                               start=True, stop=True).then_inc(S["pe_step"], 1)
            if E.name == "dve":
                for k in range(4):
                    E.e.tensor_tensor(MIXF[:, 4 + k, 0:N], MIXF[:, 4 + k, 0:N], view(H0, 4, 2 * T)[:, k, 0:N],
                                      ALU.add).then_inc(S["dve_step"], 1)
                E.e.drain()
                for j in range(8):
                    E.e.wait_ge(S["pe_step"], E.v("pe_step", j + 1))
                    E.e.scalar_tensor_tensor(out=cen[:, j, :], in0=bank[j][:, 0:N], scalar=-1.0 / C, in1=MIXF[:, j, 0:N],
                                             op0=ALU.mult, op1=ALU.add).then_inc(S["dve_step"], 1)
                for half in range(2):
                    E.e.wait_ge(S["pe_step"], E.v("pe_step", 9 + half))
                    rstd_dve(E, [(bank[4 * half][:, 0:N], var[:, half, :])], 1.0 / C, eps[half])
                for k in range(4):
                    E.e.wait_ge(S["pe_step"], E.v("pe_step", 11 + k))
                    E.e.tensor_tensor(cen[:, k, :], cen[:, k, :], bank[spread_bank[k]][:, 0:N], ALU.mult).then_inc(S["dve_step"], 1)
                for k in range(4):
                    E.e.wait_ge(S["pe_step"], E.v("pe_step", 15 + k))
                    E.e.scalar_tensor_tensor(out=cen[:, 4 + k, :], in0=bank[spread_bank[4 + k]][:, 0:N],
                                             scalar=par(l, "gng", 4)[:, k:k + 1], in1=cen[:, 4 + k, :], op0=ALU.mult, op1=ALU.mult)
                E.e.drain()
                for k in range(4):
                    E.e.scalar_tensor_tensor(out=cen[:, 4 + k, :], in0=cen[:, 4 + k, :], scalar=par(l, "gnb", 4)[:, k:k + 1],
                                             in1=US[:, k, 0:N], op0=ALU.add, op1=ALU.add)
                E.e.drain()
                for k in range(4):
                    E.e.tensor_tensor(order(MIXF[:, 4 + k, 0:N]), natural(cen[:, 4 + k, :]), natural(US[:, 4 + k, 0:N]), ALU.mult)
            if E.name == "act":
                E.e.dma_start(view(CH0 + 1024, 32 + P), a["head_rows"]).then_inc(S["layer_in"], 16)
                for j in range(8):
                    E.e.wait_ge(S["dve_step"], E.v("dve_step", 5 + j))
                    E.e.activation(sq[:, j, :], cen[:, j, :], ACT.Square).then_inc(S["act_step"], 1)
                for half in range(2):
                    E.e.wait_ge(S["dve_step"], E.v("dve_step", 13 + half))
                    E.e.activation(var[:, half, :], var[:, half, :], ACT.Sqrt).then_inc(S["act_step"], 1)
                for k in range(4):
                    E.e.wait_ge(S["dve_step"], E.v("dve_step", 15 + k))
                    E.e.activation(order(MIXF[:, k, 0:N]), natural(cen[:, k, :]), ACT.Silu,
                                   scale=par(l, "cng", 4)[:, k:k + 1], bias=par(l, "cnb", 4)[:, k:k + 1])
            E.c["layer_in"] += 16
            steps(E, pe=18, act=10, dve=18)
            phase(E)

        def gated_residual(E, l, m, N):
            def fn(u, b):
                for s in range(N // T):
                    x = XF[:, one(u), s * T:(s + 1) * T].rearrange("p o t -> p (o t)")
                    ins = E.e.scalar_tensor_tensor(out=x, in0=b[:, s * T:(s + 1) * T], scalar=MOD[l][:, one(m + u), s],
                                                   in1=x, op0=ALU.mult, op1=ALU.add)
                return ins
            return fn

        def up_down(E, N, rhs, residual):
            hid = view(R0, KF, N)
            tmp = view(CH0, 2, 512)
            if E.name == "pe":
                gemm_pe(E, 2 * KF, KD, 8, rhs, N, "free_dve", ready=("act_step", lambda k: k + 1 - KD))
            if E.name == "act":
                gated_act(E, 2 * KF, ACT.Silu, N, tmp)
            if E.name == "dve":
                gated_dve(E, 2 * KF, lambda p: hid[:, one(p), :].rearrange("p o t -> p (o t)"), N, tmp)
            units_done(E, 2 * KF, "free_dve", KF)
            if E.name == "pe":
                gemm_pe(E, KD, KF, 11, lambda k: hid[:, k, :], N, "free_dve", ready=("free_dve", lambda k: 2 * (k + 1 - KF) + 4))
            if E.name == "dve":
                take_units(E, "free_dve", KD, residual)
            units_done(E, KD, "free_dve")

        def first_layer_stages(E, l):
            N = 2 * T if l == 0 else T
            if l:
                rms_factor(E, 2 * T)
            rms_apply(E, 2 * T, lambda k, s: GS[2 * l][:, k, s:s + 1], lambda k, s: MOD[l][:, k, s:s + 1], HF)
            input_projection(E, l)
            rwkv_prep(E, l)
            recurrence(E, l == 0)
            mix_out(E, l)
            if E.name == "pe":
                gemm_pe(E, KD, KD, 8, lambda k: MIXF[:, k, 0:N], N, "free_dve")
            if E.name == "dve":
                take_units(E, "free_dve", KD, gated_residual(E, l, 16, N))
            units_done(E, KD, "free_dve")
            rms(E, N, lambda k, s: GS[2 * l + 1][:, k, s:s + 1], lambda k, s: MOD[l][:, 24 + k, s:s + 1], HF)
            up_down(E, N, lambda k: HF[:, k, 0:N], gated_residual(E, l, 40, N))

        XT = XF[:, :, 0:T]
        CUR = view(MOD0, QN + 8)
        LBND = view(MOD0 + 80, 2, 2, 4)
        lb_e = view(MOD0 + 96, 2, 4)
        lb_m = view(MOD0 + 104, 4)
        FB = view(MOD0 + 112, 4 * NB)
        F, K_, Q, I = (view(U0 + n * 1024, HH, T) for n in range(4))
        ZG, ZU, ZV = (view(U0 + n * 1024, HH, T) for n in range(4, 7))
        SZ = view(M0, 16, T)
        YB = view(R0, 64 * HB * (HB + 1) // 2)
        KE = [view(R0 + 8704 + n * 1024, 64, HB) for n in range(2)]
        PR, SU = (view(R0 + 10752 + n * 1024, 64, HB) for n in range(2))
        KH = [view(R0 + 12800 + n * 1024, HH, T) for n in range(2)]
        PS = view(CH0, HH, 2 * T)
        VT = view(CH0 + 2048, 2, 512)
        IT = view(H0, 2, 512)
        O = view(H0 + 1024, HH, T)
        ZT = view(H0 + 2048, 2, 512)
        WS = view(H0 + 3072, 4, P)
        BS = view(H0 + 3584, 4, P)
        LN_SCR = CH0 + 3072

        def blocks(v):
            return v.rearrange("p h (b j) -> p (h b) j", j=HB)

        def lower_bounds(E):
            if E.name == "dve":
                E.e.tensor_tensor(lb_m, hg_lb[:, 0, :], hg_lb[:, 1, :], ALU.max)
                E.e.drain()
                for l in range(2):
                    E.e.tensor_tensor(lb_e[:, l, :], hg_lb[:, l, :], lb_m, ALU.subtract)
                E.e.drain().then_inc(S["dve_step"], 1)
                E.e.wait_ge(S["act_step"], E.v("act_step", 1))
                E.e.tensor_tensor(lb_m, lb_e[:, 0, :], lb_e[:, 1, :], ALU.add)
                E.e.drain()
                E.e.reciprocal(lb_m, lb_m)
                E.e.drain()
                for l in range(2):
                    E.e.tensor_tensor(lb_e[:, l, :], lb_e[:, l, :], lb_m, ALU.mult)
                E.e.drain()
                E.e.tensor_tensor(LBND[:, 1, 0, :], lb_e[:, 0, :], lb_e[:, 1, :], ALU.add)
                E.e.tensor_tensor(LBND[:, 0, 0, :], lb_e[:, 0, :], lb_e[:, 0, :], ALU.subtract)
                E.e.drain()
                E.e.tensor_tensor(LBND[:, 1, 0, :], LBND[:, 1, 0, :], lb_e[:, 0, :], ALU.subtract)
                E.e.drain()
                E.e.tensor_scalar(LBND[:, :, 1, :], LBND[:, :, 0, :], -1.0, 1.0, ALU.mult, ALU.add)
            if E.name == "act":
                E.e.wait_ge(S["dve_step"], E.v("dve_step", 1))
                E.e.activation(lb_e, lb_e, ACT.Exp).then_inc(S["act_step"], 1)
            steps(E, act=1, dve=1)
            phase(E)

        def cur(name, n):
            return CUR[:, QCOL[name] + n:QCOL[name] + n + 1]

        def bound(h):
            return CUR[:, QN + h:QN + h + 1]

        def layer_start(E, l):
            if E.name == "dve":
                E.e.tensor_copy(CUR[:, 0:QN].unsqueeze(1), arena[:, P2:P2 + 2 * QN].rearrange("p (l n) -> p l n", l=2)[:, one(l), :])
                E.e.tensor_copy(CUR[:, QN:QN + 8].unsqueeze(1), LBND.rearrange("p l a b -> p l (a b)")[:, one(l), :])
            if E.name == "act":
                E.e.dma_start(WS, a["sg_ws"][one(l)].rearrange("o p g t -> p (o g) t")).then_inc(S["layer_in"], 16)
                E.e.dma_start(BS[0:1], a["sg_bs"][one(l)]).then_inc(S["layer_in"], 16)
            E.c["layer_in"] += 32
            phase(E)

        def scaled_residual(E, scale):
            def fn(u, b):
                x = XT[:, one(u), :].rearrange("p o t -> p (o t)")
                return E.e.scalar_tensor_tensor(out=x, in0=b[:, 0:T], scalar=scale, in1=x, op0=ALU.mult, op1=ALU.add)
            return fn

        def macaron(E, n, ready=None):
            hid = view(R0, KF, T)
            tmp = view(CH0, 2, 512)
            if E.name == "pe":
                gemm_pe(E, 2 * KF, KD, 8, lambda k: XT[:, k, :], T, "free_dve", ready=ready)
            if E.name == "act":
                gated_act(E, 2 * KF, ACT.Silu, T, tmp)
            if E.name == "dve":
                gated_dve(E, 2 * KF, lambda p: hid[:, one(p), :].rearrange("p o t -> p (o t)"), T, tmp)
            units_done(E, 2 * KF, "free_dve", KF)
            if E.name == "pe":
                gemm_pe(E, KD, KF, 11, lambda k: hid[:, k, :], T, "free_dve", ready=("free_dve", lambda k: 2 * (k + 1 - KF) + 4))
            if E.name == "dve":
                for k in range(KD):
                    E.e.tensor_scalar(XT[:, k, :], XT[:, k, :], ALPHA, None, ALU.mult)
                E.e.drain()
                take_units(E, "free_dve", KD, scaled_residual(E, 0.5))
            units_done(E, KD, "free_dve")
            layer_norm(E, lambda k: XT[:, k, :], lambda k: XT[:, k, :], KD,
                       lambda k: cur("lng", 8 * n + k), lambda k: cur("lnb", 8 * n + k), LN_SCR)

        def mixer_input(E):
            cen, sq, rs = view(LN_SCR, 4, T), view(LN_SCR + 4 * T, 4, T), view(LN_SCR + 8 * T, T)
            if E.name == "pe":
                def units(n, beside=None, first=False):
                    def some(i, count):
                        for u in range(count):
                            E.e.wait_ge(S["free_act"], E.v("free_act", i * 4 + u + 1))
                            w = slab_wait(E, u, i, 4)
                            for k in range(KD):
                                if first and u == 0:
                                    E.e.wait_ge(S["act_step"], E.v("act_step", k + 1 - KD))
                                    settled(E)
                                mm = E.e.matmul(bank[u][:, 0:T], w[:, k, :], XT[:, k, :], start=(k == 0), stop=(k == KD - 1))
                                if k == 0:
                                    mm.then_inc(S["slab_used"], 1)
                            mm.then_inc(S["bank_full"], 1)
                            if beside:
                                beside(i * 4 + u, u)
                    repeat(E, n, 4, some)
                    E.slab += n
                    E.c["free_act"] += n

                def block_use(half):
                    def fn(i, u):
                        n = i + 8 * half
                        E.e.wait_ge(S["dve_step"], E.v("dve_step", n))
                        for h in range(HH):
                            for x in range(half + 1):
                                mm = E.e.matmul(bank[4 + h][:, cols(n * HB + x * T, HB)], KH[u % 2][:, h, x * P:(x + 1) * P],
                                                PR[:, one(n + h * NB), :].rearrange("p o j -> p (o j)"), start=True, stop=True)
                        mm.then_inc(S["pe_step"], 1)
                    return fn
                units(4, first=True)
                units(12)
                E.e.wait_ge(S["pool_step"], E.v("pool_step", 2))
                E.e.wait_ge(S["dve_step"], E.v("dve_step", 1))
                settled(E)
                E.c["dve_step"] += 1
                units(8, block_use(0))
                units(8, block_use(1))
                E.c["dve_step"] -= 1
                E.e.wait_ge(S["act_step"], E.v("act_step", 5))
                for k in range(4):
                    mm = E.e.matmul(bank[4][:, 0:T], ones, ZV[:, k, :], start=(k == 0), stop=(k == 3))
                mm.then_inc(S["pe_step"], 1)
                units(4)
                for k in range(4):
                    E.e.wait_ge(S["act_step"], E.v("act_step", 6 + k))
                    mm = E.e.matmul(bank[5][:, 0:T], ones, sq[:, k, :], start=(k == 0), stop=(k == 3))
                mm.then_inc(S["pe_step"], 1)
                units(4)
                E.c["free_act"] -= 40
            if E.name == "act":
                def group(first, n, fn):
                    E.c["bank_full"] += first
                    E.c["free_act"] += first
                    take_units(E, "free_act", n, fn)
                    E.c["bank_full"] -= first
                    E.c["free_act"] -= first

                def forget(u, b):
                    E.e.activation(F[:, u, :], b[:, 0:T], ACT.Sigmoid)
                    return E.e.activation(K_[:, u, :], b[:, 0:T], ACT.Sigmoid, scale=-1.0)

                def into(dst, func):
                    return lambda u, b: E.e.activation(dst[:, one(u), :].rearrange("p o t -> p (o t)"), b[:, 0:T], func)
                group(0, 4, forget)
                group(4, 4, into(I, ACT.Copy))
                group(8, 4, into(Q, ACT.Copy))
                E.e.drain().then_inc(S["act_step"], 1)
                group(12, 4, into(ZG, ACT.Silu))
                group(16, 4, into(ZU, ACT.Gelu_apprx_tanh))
                group(20, 4, into(ZV, ACT.Gelu_apprx_tanh))
                group(24, 8, into(SZ, ACT.Sigmoid))
                E.e.wait_ge(S["pe_step"], E.v("pe_step", 16))
                for h in range(HH):
                    E.e.activation(PS[:, h, 0:T], bank[4 + h][:, 0:T], ACT.Copy)
                    E.e.activation(PS[:, h, T + P:2 * T], bank[4 + h][:, T + P:2 * T], ACT.Copy).then_inc(S["act_step"], 1)
                for k in range(4):
                    E.e.wait_ge(S["dve_step"], E.v("dve_step", 17 + k))
                    E.e.activation(sq[:, k, :], cen[:, k, :], ACT.Square).then_inc(S["act_step"], 1)
                group(32, 8, into(SZ[:, 8:16, :], ACT.Sigmoid))
                E.e.wait_ge(S["dve_step"], E.v("dve_step", 21))
                E.e.activation(rs, rs, ACT.Sqrt).then_inc(S["act_step"], 1)
                for k in range(4):
                    E.e.wait_ge(S["dve_step"], E.v("dve_step", 22 + k))
                    E.e.activation(ZV[:, k, :], ZV[:, k, :], ACT.Identity, bias=cur("slb", k))
            units_done(E, 40, "free_act")
            if E.name == "pool":
                for n in range(2):
                    E.e.memset(KH[n], 0.0).then_inc(S["pool_step"], 1)
                E.e.wait_ge(S["layer_in"], E.v("layer_in", 0))
                for g in range(4):
                    E.e.tensor_tensor(WS[:, g, :], WS[:, g, :], tril, ALU.mult)
            if E.name == "dve":
                E.e.wait_ge(S["act_step"], E.v("act_step", 1))
                for h in range(HH):
                    E.e.tensor_scalar(F[:, h, :], F[:, h, :], bound(4 + h), bound(h), ALU.mult, ALU.add)
                    E.e.tensor_scalar(K_[:, h, :], K_[:, h, :], bound(4 + h), None, ALU.mult)
                E.e.drain()
                f, k, q = blocks(F), blocks(K_), blocks(Q)
                E.e.tensor_copy(PR[:, :, 0:1], f[:, :, 0:1])
                E.e.memset(SU[:, :, HB - 1:HB], 1.0)
                for j in range(1, HB):
                    E.e.drain()
                    E.e.tensor_tensor(PR[:, :, j:j + 1], PR[:, :, j - 1:j], f[:, :, j:j + 1], ALU.mult)
                    E.e.tensor_tensor(SU[:, :, HB - 1 - j:HB - j], SU[:, :, HB - j:HB - j + 1], f[:, :, HB - j:HB - j + 1], ALU.mult)
                E.e.drain()
                E.e.tensor_copy(FB.unsqueeze(2), PR[:, :, HB - 1:HB])
                E.e.drain()
                E.e.tensor_tensor(PR, PR, q, ALU.mult)
                E.e.tensor_tensor(SU, SU, k, ALU.mult)
                E.e.drain().then_inc(S["dve_step"], 1)
                E.e.wait_ge(S["pool_step"], E.v("pool_step", 2))
                settled(E)

                def block_step(n, buf):
                    E.e.wait_ge(S["pe_step"], E.v("pe_step", n - 1))
                    for h in range(HH):
                        E.e.tensor_scalar(KH[buf][:, h, :], KH[1 - buf][:, h, :], FB[:, one(n - 1 + h * NB)], None, ALU.mult)
                    E.e.drain()
                    for h in range(HH):
                        ins = E.e.tensor_copy(KH[buf][:, h, cols((n - 1) * HB, HB)],
                                              SU[:, one(n - 1 + h * NB), :].rearrange("p o j -> p (o j)"))
                    ins.then_inc(S["dve_step"], 1)
                    E.e.drain()
                with E.e.Fori(0, 7) as i:
                    block_step(i * 2 + 1, 1)
                    block_step(i * 2 + 2, 0)
                block_step(15, 1)
                E.e.wait_ge(S["pe_step"], E.v("pe_step", 17))
                for c in range(4):
                    E.e.scalar_tensor_tensor(out=cen[:, c, :], in0=bank[4][:, 0:T], scalar=-1.0 / (4 * P),
                                             in1=ZV[:, c, :], op0=ALU.mult, op1=ALU.add).then_inc(S["dve_step"], 1)
                at = 0
                for lag in range(HB):
                    n = HB - lag
                    ke = KE[lag % 2]
                    if lag == 0:
                        E.e.tensor_copy(ke, k)
                    else:
                        E.e.tensor_tensor(ke[:, :, lag:HB], KE[1 - lag % 2][:, :, lag - 1:HB - 1], f[:, :, lag:HB], ALU.mult)
                    E.e.drain()
                    y = YB[:, at:at + 64 * n].rearrange("p (b j) -> p b j", j=n)
                    E.e.tensor_tensor(y, ke[:, :, lag:HB], q[:, :, lag:HB], ALU.mult)
                    at += 64 * n
                    if lag == 9:
                        E.e.wait_ge(S["pe_step"], E.v("pe_step", 18))
                        rstd_dve(E, [(bank[5][:, 0:T], rs)], 1.0 / (4 * P), LN_EPS)
                E.e.wait_ge(S["act_step"], E.v("act_step", 10))
                for c in range(4):
                    E.e.scalar_tensor_tensor(out=ZV[:, c, :], in0=cen[:, c, :], scalar=cur("slg", c), in1=rs,
                                             op0=ALU.mult, op1=ALU.mult).then_inc(S["dve_step"], 1)
            steps(E, pe=18, act=10, dve=25, pool=2)
            phase(E)

        def spatial_gate(E):
            if E.name == "pe":
                for x, src in ((0, ZV), (1, I)):
                    for n in range(2):
                        for g in range(4):
                            mm = E.e.transpose(bank[2 * x + n][:, g * P:(g + 1) * P], src[:, g, n * P:(n + 1) * P], ident)
                        mm.then_inc(S["pe_step"], 1)
                E.e.wait_ge(S["layer_in"], E.v("layer_in", 0))
                E.e.wait_ge(S["act_step"], E.v("act_step", 2))
                for g in range(4):
                    for n in range(2):
                        o = bank[4 + g // 2][:, (g % 2) * T + n * P:(g % 2) * T + (n + 1) * P]
                        E.e.matmul(o, VT[:, n, g * P:(g + 1) * P], WS[:, g, :], start=True, stop=False)
                        mm = E.e.matmul(o, ones[0:1, :], BS[0:1, g, :], start=False, stop=True)
                mm.then_inc(S["pe_step"], 1)
            if E.name == "act":
                for n in range(4):
                    E.e.wait_ge(S["pe_step"], E.v("pe_step", n + 1))
                    E.e.activation((VT if n < 2 else IT)[:, n % 2, :], bank[n][:, :], ACT.Copy).then_inc(S["act_step"], 1)
            if E.name == "dve":
                E.e.wait_ge(S["pe_step"], E.v("pe_step", 5))
                for x in range(2):
                    u = ZU[:, 2 * x:2 * x + 2, :].rearrange("p h t -> p (h t)")
                    E.e.tensor_tensor(u, u, bank[4 + x][:, :], ALU.mult)
            steps(E, pe=5, act=4)
            phase(E)

        def hgrn(E):
            if E.name == "pe":
                for h in range(HH):
                    o = (h % 2) * T
                    E.e.matmul(bank[h // 2][:, o:o + T], IT[:, 0, h * P:(h + 1) * P], PS[:, h, 0:T],
                               start=True, stop=False, skip_group_check=True)
                    mm = E.e.matmul(bank[h // 2][:, o + P:o + T], IT[:, 1, h * P:(h + 1) * P], PS[:, h, T + P:2 * T],
                                    start=False, stop=True, skip_group_check=True)
                mm.then_inc(S["pe_step"], 1)
                at, u = 0, 0
                for lag in range(HB):
                    n = 32 * (HB - lag)
                    for x in range(2):
                        if u >= 2:
                            E.e.wait_ge(S["dve_step"], E.v("dve_step", u - 1))
                        E.e.matmul(bank[2 + x][:, 0:n], ones, YB[:, at:at + n], start=True, stop=True).then_inc(S["pe_step"], 1)
                        at += n
                        u += 1
                    if lag % 2 == 0:
                        v = lag // 2
                        E.e.wait_ge(S["free_dve"], E.v("free_dve", v + 1))
                        w = slab_wait(E, v // 2, 0, 4)
                        for k in range(4):
                            mm = E.e.matmul(bank[4 + v % 4][:, 0:T], w[:, v % 2 * 4 + k, :], ZU[:, k, :],
                                            start=(k == 0), stop=(k == 3))
                            if k == 0 and v % 2 == 0:
                                mm.then_inc(S["slab_used"], 1)
                        mm.then_inc(S["bank_full"], 1)
                E.slab += 4
            if E.name == "dve":
                i = blocks(I)
                o = blocks(O)
                u = 0
                for lag in range(HB):
                    n = HB - lag
                    for x in range(2):
                        E.e.wait_ge(S["pe_step"], E.v("pe_step", 2 + u))
                        b = bank[2 + x][:, 0:32 * n].rearrange("p (b j) -> p b j", j=n)
                        bs = slice(32 * x, 32 * x + 32)
                        z = (o if lag == 0 else ZT[:, x, :].rearrange("p (b j) -> p b j", j=HB))
                        z = z[:, bs, :] if lag == 0 else z[:, :, 0:n]
                        E.e.tensor_tensor(z, b, i[:, bs, 0:n], ALU.mult).then_inc(S["dve_step"], 1)
                        u += 1
                    E.e.drain()
                    if lag:
                        for x in range(2):
                            bs = slice(32 * x, 32 * x + 32)
                            z = ZT[:, x, :].rearrange("p (b j) -> p b j", j=HB)[:, :, 0:n]
                            E.e.tensor_tensor(o[:, bs, lag:HB], o[:, bs, lag:HB], z, ALU.add)
                        E.e.drain()
                    if lag % 2 == 1:
                        v = lag // 2
                        E.e.wait_ge(S["bank_full"], E.v("bank_full", v + 1))
                        E.e.tensor_tensor(SZ[:, 8 + v, :], SZ[:, 8 + v, :], bank[4 + v % 4][:, 0:T],
                                          ALU.mult).then_inc(S["free_dve"], 1)
                for x in range(2):
                    oo = O[:, 2 * x:2 * x + 2, :].rearrange("p h t -> p (h t)")
                    E.e.tensor_tensor(oo, oo, bank[x][:, :], ALU.add)
            units_done(E, KD, "free_dve")
            steps(E, pe=33, dve=32)
            phase(E)
            if E.name == "act":
                for x in range(2):
                    E.e.activation(ZT[:, x, :], O[:, 2 * x:2 * x + 2, :].rearrange("p h t -> p (h t)"), ACT.Square).then_inc(S["act_step"], 1)
                for x in range(2):
                    E.e.wait_ge(S["dve_step"], E.v("dve_step", x + 1))
                    E.e.activation(ZT[:, x, :], ZT[:, x, :], ACT.Sqrt).then_inc(S["act_step"], 1)
            if E.name == "pe":
                for x in range(2):
                    E.e.wait_ge(S["act_step"], E.v("act_step", x + 1))
                    E.e.matmul(bank[x][:, :], ones, ZT[:, x, :], start=True, stop=True).then_inc(S["pe_step"], 1)
            if E.name == "dve":
                E.e.wait_ge(S["pe_step"], E.v("pe_step", 2))
                rstd_dve(E, [(bank[x][:, :], ZT[:, x, :]) for x in range(2)], 1.0 / P, RMS_EPS)
                E.e.wait_ge(S["act_step"], E.v("act_step", 4))
                for h in range(HH):
                    E.e.scalar_tensor_tensor(out=O[:, h, :], in0=O[:, h, :], scalar=cur("ng", h),
                                             in1=ZT[:, h // 2, (h % 2) * T:(h % 2 + 1) * T], op0=ALU.mult, op1=ALU.mult)
                E.e.drain()
                E.e.tensor_tensor(O.rearrange("p h t -> p (h t)"), O.rearrange("p h t -> p (h t)"),
                                  ZG.rearrange("p h t -> p (h t)"), ALU.mult)
            steps(E, pe=2, act=4, dve=2)
            phase(E)

        def mixer_output(E):
            if E.name == "pe":
                gemm_pe(E, KD, 4, 8, lambda k: O[:, k, :], T, "free_dve", body=8)
            if E.name == "dve":
                def fn(u, b):
                    return E.e.tensor_tensor(SZ[:, u, :], SZ[:, u, :], b[:, 0:T], ALU.mult)
                take_units(E, "free_dve", KD, fn, body=8)
            units_done(E, KD, "free_dve")
            if E.name == "dve":
                E.e.drain()
                for k in range(KD):
                    E.e.tensor_tensor(SZ[:, k, :], SZ[:, k, :], SZ[:, 8 + k, :], ALU.add).then_inc(S["dve_step"], 1)
                for k in range(KD):
                    E.e.tensor_scalar(XT[:, k, :], XT[:, k, :], ALPHA, None, ALU.mult)
                E.e.drain()
            steps(E, dve=KD)
            if E.name == "pe":
                gemm_pe(E, KD, KD, 8, lambda k: SZ[:, k, :], T, "free_dve", ready=("dve_step", lambda k: k + 1 - KD))
            if E.name == "dve":
                take_units(E, "free_dve", KD, scaled_residual(E, 1.0))
            units_done(E, KD, "free_dve")
            layer_norm(E, lambda k: XT[:, k, :], lambda k: XT[:, k, :], KD,
                       lambda k: cur("lng", 8 + k), lambda k: cur("lnb", 8 + k), LN_SCR)

        def program(E):
            if E.name == "pe":
                E.e.drain().then_inc(S["slab_used"], RING - 1)
            if E.name == "dve":
                E.e.drain().then_inc(S["free_dve"], 4)
            if E.name == "act":
                E.e.drain().then_inc(S["free_act"], 4)
            E.e.wait_ge(S["consts_in"], 16 * 4)
            modulation_start(E)
            for l in range(DEPTH):
                first_layer_stages(E, l)
            rms(E, T, lambda k, s: final_g[:, k:k + 1], None, XF)
            lower_bounds(E)
            before = dict(E.c)
            slab = E.slab
            with E.e.Fori(0, DEPTH) as l:
                E.l = l
                layer_start(E, l)
                macaron(E, 0)
                mixer_input(E)
                spatial_gate(E)
                hgrn(E)
                mixer_output(E)
                macaron(E, 2, ready=("act_step", lambda k: k + 1 - KD))
                phase(E)
            E.l = None
            grown = {k: E.c[k] - before[k] for k in E.c}
            assert grown == PER, grown
            for k in E.c:
                E.c[k] = before[k] + DEPTH * PER[k]
            assert E.name != "pe" or E.slab - slab == SLABS2, E.slab - slab

        block = ctx.enter_context(nc.Block())

        @block.sync
        def _(sp):
            E = Eng(sp, "sp")
            sp.dma_start(cst, a["consts"]).then_inc(S["consts_in"], 16)
            sp.dma_start(arena[:, K0:K1], a["params"]).then_inc(S["consts_in"], 16)
            sp.dma_start(cond, a["cond"]).then_inc(S["consts_in"], 16)
            sp.dma_start(X, a["x"]).then_inc(S["consts_in"], 16)

            def rows_of(name, per):
                def src(at):
                    at = at if E.l is None else at + E.l * per
                    return a[name][one(at)].rearrange("o p w -> p (o w)")
                return src
            load_slabs(E, rows_of("ada_w", 0), ADA_FIRST, 8)
            for l in range(DEPTH):
                w_in, ada = rows_of("w_in", 0), rows_of("ada_w", 0)
                if l == 0:
                    def some(i, count):
                        for s in range(count):
                            u, x = divmod(s, 5)
                            if x in (0, 2):
                                slab_to_slot(E, s, i, 20, w_in(i * 4 + u)[:, 256 * x:256 * x + 512], 4 * P)
                            else:
                                slab_to_slot(E, s, i, 20, ada(i * 12 + (ADA_FIRST + 3 * u + x - 1 - (x > 2))), 8 * P)
                    repeat(E, 5 * 23, 20, some)
                    E.slab += 5 * 23
                else:
                    load_slabs(E, w_in, 23, 8, first=23)
                load_slabs(E, rows_of("w_out", 0), 8, 8, first=8 * l)
                load_slabs(E, rows_of("ffn_up", 0), 44, 8, first=44 * l)
                load_slabs(E, rows_of("ffn_down", 0), 16, 11, first=16 * l)
            with sp.Fori(0, DEPTH) as l:
                E.l = l
                load_slabs(E, rows_of("ffn1_up", 44), 44, 8)
                load_slabs(E, rows_of("ffn1_down", 16), 16, 11)
                load_slabs(E, rows_of("w_in_2", 40), 40, 8)
                load_slabs(E, rows_of("branches", 8), 8, 8)
                load_slabs(E, rows_of("w_out_2", 8), 8, 8)
                load_slabs(E, rows_of("ffn2_up", 44), 44, 8)
                load_slabs(E, rows_of("ffn2_down", 16), 16, 11)
            sp.wait_ge(S["store"], 1)
            sp.dma_start(out, XT).then_inc(S["x_in"], 16)
            sp.wait_ge(S["x_in"], 16)

        @block.tensor
        def _(pe):
            program(Eng(pe, "pe"))

        @block.scalar
        def _(act):
            program(Eng(act, "act"))
            act.drain().then_inc(S["store"], 1)

        @block.vector
        def _(dve):
            program(Eng(dve, "dve"))

        @block.gpsimd
        def _(pool):
            program(Eng(pool, "pool"))


PER = {"slab_used": 0, "bank_full": 168, "free_dve": 128, "free_act": 40, "act_ready": 44, "pe_phase": 6,
       "act_phase": 6, "dve_phase": 6, "pool_phase": 6, "pe_step": 64, "act_step": 69, "dve_step": 118,
       "pool_step": 2, "consts_in": 0, "layer_in": 32, "x_in": 0, "store": 0, "ada_full": 0, "ada_copied": 0}


def slabs(w, order, K, tiles):
    L, rows, N = w.shape
    n = len(order)
    pad = (max(order) + 1) * P - N
    if pad > 0:
        w = np.concatenate([w, np.zeros((L, rows, pad), w.dtype)], axis=2)
    t = w.reshape(L, K, P, w.shape[2] // P, P)[:, :, :, list(order), :]
    t = t.transpose(0, 3, 1, 2, 4).reshape(L * n * K // tiles, tiles, P, P)
    return np.ascontiguousarray(t.transpose(0, 2, 1, 3)).reshape(L * n * K // tiles, P, tiles * P)


def feature_columns(v, n):
    v = v.reshape(-1, v.shape[-1])
    pad = -v.shape[1] % P
    if pad:
        v = np.concatenate([v, np.zeros((v.shape[0], pad), v.dtype)], axis=1)
    return v.reshape(v.shape[0], -1, P)


def constants():
    s, t = np.arange(P)[:, None], np.arange(P)[None, :]
    out = {"ident": np.eye(P), "ones": np.ones((P, P)), "blk64": s // C == t // C}
    same = s // C == t // C
    sl, tl = s % C, t % C
    half = C // 2
    cum = np.zeros((P, 2, 2, P))
    cum[:, 0, 0] = same * ((sl <= tl) * 1.0 - (sl < half))
    cum[:, 0, 1] = same * ((sl < tl) * 1.0 - (sl < half))
    cum[:, 1, 0] = same * ((sl >= tl) * 1.0 - (sl >= half))
    cum[:, 1, 1] = same * ((sl > tl) * 1.0 - (sl >= half))
    out["cum"] = cum
    s1 = np.arange(P)[:, None] % C
    t1 = np.arange(C)[None, :]
    m1 = np.zeros((P, 2, P))
    m1[:, 0, :C], m1[:, 0, C:] = s1 < t1, s1 <= t1
    m1[:, 1, :C], m1[:, 1, C:] = s1 > t1, s1 >= t1
    out["m1"] = m1
    inv = np.zeros((P, 2, LEVELS, C))
    for lv in range(LEVELS):
        b = 1 << lv
        both = s1 // (2 * b) == t1 // (2 * b)
        inv[:, 0, lv] = both & (s1 // b % 2 == 0) & (t1 // b % 2 == 1)
        inv[:, 1, lv] = both & (s1 // b % 2 == 1) & (t1 // b % 2 == 0)
    out["inv"] = inv
    neg0 = np.zeros((P, 2, 2, C))
    for d in range(2):
        neg0[:, d, 0], neg0[:, d, 1] = -inv[:, d, 0], -inv[:, 1 - d, 0]
    out["neg0"] = neg0
    out["eye64"] = s1 == t1
    out["tril"] = s <= t
    out["pick"] = s % 32 == np.arange(2)[None, :]
    return np.concatenate([np.asarray(out[n], np.float32).reshape(P, -1) for n, _ in CONSTS], axis=1)


def kernel(**x):
    import concourse.bacc as bacc
    from concourse.bass_utils import run_bass_kernel_spmd

    x = {k: np.ascontiguousarray(v) for k, v in x.items()}
    ff = [j for p in range(KF) for j in (p, KF + p)]
    joined = np.concatenate([x["ffn_wg"], x["ffn_wu"]], axis=2)
    arrays = {
        "consts": constants(),
        "ada_w": slabs(x["ada_w"], range(48), KD, 8),
        "w_in": slabs(x["w_in"], [j for p in range(4) for j in (4 + p, p)] + list(range(8, 23)), KD, 8),
        "w_out": slabs(x["w_out"], range(8), KD, 8),
        "ffn_up": slabs(joined, ff, KD, 8),
        "ffn_down": slabs(x["ffn_wd"], range(8), KF, 11),
        "ffn1_up": slabs(x["ffn1_w13_2"], ff, KD, 8),
        "ffn1_down": slabs(x["ffn1_w2_2"], range(8), KF, 11),
        "ffn2_up": slabs(x["ffn2_w13_2"], ff, KD, 8),
        "ffn2_down": slabs(x["ffn2_w2_2"], range(8), KF, 11),
        "w_in_2": slabs(x["w_in_2"], [*range(4, 8), *range(8, 12), *range(0, 4), *range(12, 40)], KD, 8),
        "w_out_2": slabs(x["w_out_2"], range(8), KD, 8),
    }
    br = [slabs(x[n], range(8), 4, 8).reshape(DEPTH, 4, P, 8 * P) for n in ("w_branch_b_2", "w_branch_a_2")]
    arrays["branches"] = np.stack(br, axis=1).reshape(DEPTH * 8, P, 8 * P)
    xs = np.stack([x["x"][0], x["ctx"][0]])
    arrays["x"] = np.ascontiguousarray(xs.reshape(2, T, KD, P).transpose(3, 2, 0, 1))
    arrays["cond"] = np.ascontiguousarray(np.stack([x["c"][0], x["c_ctx"]]).reshape(2, KD, P).transpose(2, 1, 0))

    def chunked(v):
        return feature_columns(v, 0).transpose(2, 0, 1)

    cols_ = []
    for l in range(DEPTH):
        one = {"n1g": x["norm1_g"][l], "n2g": x["norm2_g"][l], "cb": x["conv_b"][l], "cng": x["cnorm_g"][l],
               "cnb": x["cnorm_b"][l], "ib0": x["iclr_b0"][l], "kk": x["k_k"][l], "ka": x["k_a"][l],
               "rk": x["r_k"][l], "gng": x["gn_g"][l], "gnb": x["gn_b"][l], "adab": x["ada_b"][l]}
        parts = {n: chunked(v).reshape(P, -1) for n, v in one.items()}
        parts["cw"] = chunked(x["conv_w"][l]).transpose(0, 2, 1).reshape(P, -1)
        parts["sw"] = chunked(x["shift_w"][l]).transpose(0, 2, 1).reshape(P, -1)
        cols_ += [parts[n] for n, k in PARAMS1 if k]
    cols_.append(chunked(x["final_g"]).reshape(P, -1))
    for l in range(DEPTH):
        parts = {"lng": x["ln_g_2"][l], "lnb": x["ln_b_2"][l], "ng": x["hg_norm_g_2"][l],
                 "slg": x["sg_ln_g_2"][l], "slb": x["sg_ln_b_2"][l]}
        cols_ += [chunked(parts[n]).reshape(P, -1) for n, _ in PARAMS2]
    cols_.append(chunked(x["hg_lb_2"]).reshape(P, -1))
    arrays["params"] = np.ascontiguousarray(np.concatenate(cols_, axis=1))
    arrays["decay_w"] = np.concatenate([x["decay_up"], x["decay_b0"][:, :, None, :]], axis=2).transpose(0, 2, 1, 3).reshape(DEPTH, 65, 1024)
    arrays["iclr_w"] = x["iclr_up"].transpose(0, 2, 1, 3).reshape(DEPTH, 64, 1024)
    g = np.concatenate([x["g_up"], np.zeros((DEPTH, 96, 512), np.float32)], axis=1)
    arrays["gate_w"] = g.reshape(DEPTH, 2, P, 512).transpose(0, 2, 1, 3)
    arrays["sg_ws"] = x["sg_ws_2"].transpose(0, 3, 1, 2)
    arrays["sg_bs"] = x["sg_bs_2"].reshape(DEPTH, 4, P)

    s = np.arange(P)[:, None]
    arrays["head_rows"] = np.concatenate([s // C == np.arange(32)[None, :], s % 32 == np.arange(P)[None, :] // C],
                                         axis=1).astype(np.float32)

    nc = bacc.Bacc("TRN2", target_bir_lowering=False, num_devices=1)
    ins = {}
    for n, v in arrays.items():
        arrays[n] = np.ascontiguousarray(v)
        ins[n] = nc.dram_tensor("in_" + n, v.shape, mybir.dt.from_np(v.dtype), kind="ExternalInput").ap()
    out = nc.dram_tensor("out_x", (P, KD, T), F32, kind="ExternalOutput").ap()
    build(nc, ins, out)
    r = run_bass_kernel_spmd(nc, [{"in_" + n: v for n, v in arrays.items()}], core_ids=[0])
    y = r.results[0]["out_x"]
    return np.ascontiguousarray(y.transpose(2, 1, 0)).reshape(1, T, D)
```
